# Optimizing a Trainium2 kernel written in Bass

```python
import jax, jax.numpy as jnp
from jax import lax
import numpy as np

D_MODEL = 1024
BATCH = 1
SEQ = 128
DEPTH = 2
DEC_BATCH = 1
DEC_SEQ = 512
PAST_LEN = 128

GRID_W = 64
N_MIXERS = 2
N_RET = (DEPTH + 1) // 2
N_ATTN = DEPTH // 2
RET_HEADS = 4
RET_DK = 256
RET_DV = 512
RET_CHUNK = 128
ATTN_HEADS = 16
ATTN_KV_HEADS = 4
ATTN_GROUPS = ATTN_HEADS // ATTN_KV_HEADS
HEAD_DIM = 64
WINDOW = 128
ATTN_BLOCK = 128
D_FF = 2816
CONV_WIDTH = 3
ROPE_BASE = 10000.0
EPS = 1e-6
N_MOD = 6
NEG_INF = -1e30

kernel_name = "hybrid_retention_swa_prefix_dit_step"

def rmsnorm(x, g):
    xf = x.astype(jnp.float32)
    y = xf * lax.rsqrt(jnp.mean(xf * xf, axis=-1, keepdims=True) + EPS)
    return y.astype(x.dtype) * g

def head_rms(x):
    xf = x.astype(jnp.float32)
    return (xf * lax.rsqrt(jnp.mean(xf * xf, axis=-1, keepdims=True) + EPS)).astype(x.dtype)

def adaln(cvec, w, b):
    m = jax.nn.silu(cvec) @ w + b
    return jnp.split(m, N_MOD, axis=-1)

def modulate(x, g, shift, scale):
    return rmsnorm(x, g) * (1.0 + scale) + shift

def rope_half(x, pos):
    n_freq = x.shape[-1] // 2
    inv = ROPE_BASE ** (-jnp.arange(n_freq, dtype=jnp.float32) / n_freq)
    ang = pos.astype(jnp.float32)[:, None] * inv[None, :]
    cos = jnp.cos(ang)[None, :, None, :].astype(x.dtype)
    sin = jnp.sin(ang)[None, :, None, :].astype(x.dtype)
    x1, x2 = x[..., :n_freq], x[..., n_freq:]
    return jnp.concatenate([x1 * cos - x2 * sin, x1 * sin + x2 * cos], axis=-1)

def axial_rope(x):
    L = x.shape[1]
    n_rows = L // GRID_W
    rows = jnp.repeat(jnp.arange(n_rows), GRID_W)
    cols = jnp.tile(jnp.arange(GRID_W), n_rows)
    half = x.shape[-1] // 2
    return jnp.concatenate([rope_half(x[..., :half], rows), rope_half(x[..., half:], cols)], axis=-1)

def retention_scan(q, k, v, log_gamma, s0):
    B, L, H, DK = q.shape
    DV = v.shape[-1]
    C = RET_CHUNK
    n = L // C
    idx = jnp.arange(C, dtype=jnp.float32)
    lg = log_gamma[:, None]
    diff = idx[:, None] - idx[None, :]
    dmat = jnp.where(diff >= 0, jnp.exp(lg[:, :, None] * jnp.maximum(diff, 0.0)), 0.0).astype(q.dtype)
    xi = jnp.exp(lg * (idx + 1.0)).T.astype(q.dtype)
    zeta = jnp.exp(lg * (C - 1.0 - idx)).T.astype(q.dtype)
    g_chunk = jnp.exp(log_gamma * C).astype(q.dtype)

    def to_chunks(t):
        return t.reshape(B, n, C, H, t.shape[-1]).transpose(1, 0, 2, 3, 4)

    def step(S, inp):
        qc, kc, vc = inp
        s = jnp.einsum('bihd,bjhd->bhij', qc, kc) * dmat[None]
        inner = jnp.einsum('bhij,bjhv->bihv', s, vc)
        cross = jnp.einsum('bihd,bhdv->bihv', qc, S) * xi[None, :, :, None]
        S_new = S * g_chunk[None, :, None, None] + jnp.einsum('bjhd,bjhv->bhdv', kc * zeta[None, :, :, None], vc)
        return S_new, inner + cross

    s_fin, out = lax.scan(step, s0.astype(q.dtype), (to_chunks(q), to_chunks(k), to_chunks(v)))
    return out.transpose(1, 0, 2, 3, 4).reshape(B, L, H, DV), s_fin

def retention_direction(q, k, v, log_gamma, s0, reverse):
    if reverse:
        o, s = retention_scan(q[:, ::-1], k[:, ::-1], v[:, ::-1], log_gamma, s0)
        return o[:, ::-1], s
    return retention_scan(q, k, v, log_gamma, s0)

def retention_mixer(h, wq, wk, wv, wg_f, wg_b, wo, raw_f, raw_b, s0_f, s0_b, rope):
    B, L, _ = h.shape
    q = (h @ wq).reshape(B, L, RET_HEADS, RET_DK)
    k = (h @ wk).reshape(B, L, RET_HEADS, RET_DK) * (RET_DK ** -0.5)
    v = (h @ wv).reshape(B, L, RET_HEADS, RET_DV)
    if rope:
        q, k = axial_rope(q), axial_rope(k)
    lg_f = jax.nn.log_sigmoid(raw_f.astype(jnp.float32))
    lg_b = jax.nn.log_sigmoid(raw_b.astype(jnp.float32))
    o_f, s_f = retention_direction(q, k, v, lg_f, s0_f, False)
    o_b, s_b = retention_direction(q, k, v, lg_b, s0_b, True)
    y = (head_rms(o_f).reshape(B, L, RET_HEADS * RET_DV) * jax.nn.silu(h @ wg_f)
         + head_rms(o_b).reshape(B, L, RET_HEADS * RET_DV) * jax.nn.silu(h @ wg_b))
    return y @ wo, s_f, s_b

def attn_project(h, wq, wk, wv):
    B, L, _ = h.shape
    q = (h @ wq).reshape(B, L, ATTN_HEADS, HEAD_DIM)
    k = (h @ wk).reshape(B, L, ATTN_KV_HEADS, HEAD_DIM)
    v = (h @ wv).reshape(B, L, ATTN_KV_HEADS, HEAD_DIM)
    return q, k, v

def softmax_with_sink(logits, sink):
    sink_col = jnp.broadcast_to(sink.astype(jnp.float32).reshape(ATTN_KV_HEADS, ATTN_GROUPS, 1, 1),
                                logits.shape[:-1] + (1,))
    p = jax.nn.softmax(jnp.concatenate([logits, sink_col], axis=-1), axis=-1)
    return p[..., :-1]

def context_attention(q, k, v, sink):
    B, L, H, D = q.shape
    n = L // ATTN_BLOCK
    scale = D ** -0.5
    qb = q.reshape(B, n, ATTN_BLOCK, ATTN_KV_HEADS, ATTN_GROUPS, D).transpose(1, 0, 2, 3, 4, 5)

    def block(qi):
        s = jnp.einsum('bqkgd,bskd->bkgqs', qi, k).astype(jnp.float32) * scale
        p = softmax_with_sink(s, sink).astype(v.dtype)
        return jnp.einsum('bkgqs,bskd->bqkgd', p, v)

    out = lax.map(block, qb)
    return out.transpose(1, 0, 2, 3, 4, 5).reshape(B, L, H * D)

def latent_attention(q, k, v, k_ctx, v_ctx, sink):
    B, L, H, D = q.shape
    blk = ATTN_BLOCK
    n = L // blk
    scale = D ** -0.5
    qb = q.reshape(B, n, blk, ATTN_KV_HEADS, ATTN_GROUPS, D)

    def band(t):
        z = jnp.zeros((B, blk) + t.shape[2:], t.dtype)
        tp = jnp.concatenate([z, t, z], axis=1).reshape(B, n + 2, blk, ATTN_KV_HEADS, D)
        return jnp.concatenate([tp[:, :-2], tp[:, 1:-1], tp[:, 2:]], axis=2)

    kb, vb = band(k), band(v)
    qpos = jnp.arange(L).reshape(n, blk)
    kpos = (jnp.arange(n)[:, None] - 1) * blk + jnp.arange(3 * blk)[None, :]
    rel = qpos[:, :, None] - kpos[:, None, :]
    valid = (jnp.abs(rel) <= WINDOW) & (kpos[:, None, :] >= 0) & (kpos[:, None, :] < L)
    s_band = jnp.einsum('bnqkgd,bnskd->bnkgqs', qb, kb).astype(jnp.float32) * scale
    s_band = jnp.where(valid[None, :, None, None], s_band, NEG_INF)
    s_ctx = jnp.einsum('bnqkgd,bskd->bnkgqs', qb, k_ctx).astype(jnp.float32) * scale
    p = softmax_with_sink(jnp.concatenate([s_band, s_ctx], axis=-1), sink).astype(v.dtype)
    nb = 3 * blk
    out = (jnp.einsum('bnkgqs,bnskd->bnqkgd', p[..., :nb], vb)
           + jnp.einsum('bnkgqs,bskd->bnqkgd', p[..., nb:], v_ctx))
    return out.reshape(B, L, H * D)

def conv_ffn(h, w_in, conv_w, conv_b, w_out):
    a = h @ w_in
    L = a.shape[1]
    ap = jnp.pad(a, ((0, 0), (1, 1), (0, 0)))
    a = ap[:, :L] * conv_w[0] + ap[:, 1:L + 1] * conv_w[1] + ap[:, 2:] * conv_w[2] + conv_b
    u, g = jnp.split(a, 2, axis=-1)
    return (jax.nn.silu(g) * u) @ w_out

def setup_inputs(seed: int = 0) -> dict:
    key = jax.random.key(seed)
    ks = jax.random.split(key, 40)

    def nrm(k, shape, scale=1.0):
        return jax.random.normal(k, shape, jnp.float32) * scale

    D = D_MODEL
    gamma0 = 1.0 - jnp.exp(jnp.linspace(jnp.log(1.0 / 32.0), jnp.log(1.0 / 512.0), RET_HEADS))
    raw0 = jnp.log(gamma0 / (1.0 - gamma0)).astype(jnp.float32)
    return {
        "x_prompt": nrm(ks[0], (BATCH, SEQ, D)),
        "x_sample": nrm(ks[1], (DEC_BATCH, DEC_SEQ, D)),
        "state_ret_fwd": nrm(ks[2], (DEC_BATCH, N_RET, RET_HEADS, RET_DK, RET_DV), 0.5),
        "state_ret_bwd": nrm(ks[3], (DEC_BATCH, N_RET, RET_HEADS, RET_DK, RET_DV), 0.5),
        "cache_attn_k": nrm(ks[4], (DEC_BATCH, N_ATTN, PAST_LEN, ATTN_KV_HEADS, HEAD_DIM)),
        "cache_attn_v": nrm(ks[5], (DEC_BATCH, N_ATTN, PAST_LEN, ATTN_KV_HEADS, HEAD_DIM)),
        "c": nrm(ks[6], (DEC_BATCH, D)),
        "c_ctx": nrm(ks[7], (D,)),
        "ada_w": nrm(ks[8], (DEPTH, D, N_MOD * D), D ** -0.5),
        "ada_b": nrm(ks[9], (DEPTH, N_MOD * D), 0.02),
        "norm_mix": 1.0 + nrm(ks[10], (DEPTH, D), 0.02),
        "norm_ffn": 1.0 + nrm(ks[11], (DEPTH, D), 0.02),
        "ret_wq": nrm(ks[12], (N_RET, D, RET_HEADS * RET_DK), D ** -0.5),
        "ret_wk": nrm(ks[13], (N_RET, D, RET_HEADS * RET_DK), D ** -0.5),
        "ret_wv": nrm(ks[14], (N_RET, D, RET_HEADS * RET_DV), D ** -0.5),
        "ret_wg_fwd": nrm(ks[15], (N_RET, D, RET_HEADS * RET_DV), D ** -0.5),
        "ret_wg_bwd": nrm(ks[16], (N_RET, D, RET_HEADS * RET_DV), D ** -0.5),
        "ret_wo": nrm(ks[17], (N_RET, RET_HEADS * RET_DV, D), (RET_HEADS * RET_DV) ** -0.5),
        "ret_decay_fwd": raw0[None, :] + nrm(ks[18], (N_RET, RET_HEADS), 0.01),
        "ret_decay_bwd": raw0[None, :] + nrm(ks[19], (N_RET, RET_HEADS), 0.01),
        "attn_wq": nrm(ks[20], (N_ATTN, D, ATTN_HEADS * HEAD_DIM), D ** -0.5),
        "attn_wk": nrm(ks[21], (N_ATTN, D, ATTN_KV_HEADS * HEAD_DIM), D ** -0.5),
        "attn_wv": nrm(ks[22], (N_ATTN, D, ATTN_KV_HEADS * HEAD_DIM), D ** -0.5),
        "attn_wo": nrm(ks[23], (N_ATTN, ATTN_HEADS * HEAD_DIM, D), (ATTN_HEADS * HEAD_DIM) ** -0.5),
        "attn_sink": nrm(ks[24], (N_ATTN, ATTN_HEADS), 0.5),
        "ffn_w_in": nrm(ks[25], (DEPTH, D, 2 * D_FF), D ** -0.5),
        "ffn_conv_w": nrm(ks[26], (DEPTH, CONV_WIDTH, 2 * D_FF), CONV_WIDTH ** -0.5),
        "ffn_conv_b": nrm(ks[27], (DEPTH, 2 * D_FF), 0.02),
        "ffn_w_out": nrm(ks[28], (DEPTH, D_FF, D), D_FF ** -0.5),
        "norm_final": 1.0 + nrm(ks[29], (D,), 0.02),
    }

def reference(x_prompt, x_sample, state_ret_fwd, state_ret_bwd, cache_attn_k, cache_attn_v, c, c_ctx,
              ada_w, ada_b, norm_mix, norm_ffn,
              ret_wq, ret_wk, ret_wv, ret_wg_fwd, ret_wg_bwd, ret_wo, ret_decay_fwd, ret_decay_bwd,
              attn_wq, attn_wk, attn_wv, attn_wo, attn_sink,
              ffn_w_in, ffn_conv_w, ffn_conv_b, ffn_w_out, norm_final):
    xc, xl = x_prompt, x_sample
    b_ctx = xc.shape[0]
    new_sf, new_sb, new_k, new_v = [], [], [], []
    for l in range(DEPTH):
        mc = adaln(c_ctx, ada_w[l], ada_b[l])
        ml = [t[:, None, :] for t in adaln(c, ada_w[l], ada_b[l])]
        hc = modulate(xc, norm_mix[l], mc[0], mc[1])
        hl = modulate(xl, norm_mix[l], ml[0], ml[1])
        if l % N_MIXERS == 0:
            r = l // N_MIXERS
            w = (ret_wq[r], ret_wk[r], ret_wv[r], ret_wg_fwd[r], ret_wg_bwd[r], ret_wo[r],
                 ret_decay_fwd[r], ret_decay_bwd[r])
            zero = jnp.zeros((b_ctx, RET_HEADS, RET_DK, RET_DV), xc.dtype)
            yc, s_f, s_b = retention_mixer(hc, *w, zero, zero, rope=False)
            yl, _, _ = retention_mixer(hl, *w, state_ret_fwd[:, r], state_ret_bwd[:, r], rope=True)
            new_sf.append(s_f)
            new_sb.append(s_b)
        else:
            a = l // N_MIXERS
            qc, kc, vc = attn_project(hc, attn_wq[a], attn_wk[a], attn_wv[a])
            yc = context_attention(qc, kc, vc, attn_sink[a]) @ attn_wo[a]
            ql, kl, vl = attn_project(hl, attn_wq[a], attn_wk[a], attn_wv[a])
            yl = latent_attention(axial_rope(ql), axial_rope(kl), vl,
                                  cache_attn_k[:, a], cache_attn_v[:, a], attn_sink[a]) @ attn_wo[a]
            new_k.append(kc)
            new_v.append(vc)
        xc = xc + mc[2] * yc
        xl = xl + ml[2] * yl
        hc = modulate(xc, norm_ffn[l], mc[3], mc[4])
        hl = modulate(xl, norm_ffn[l], ml[3], ml[4])
        xc = xc + mc[5] * conv_ffn(hc, ffn_w_in[l], ffn_conv_w[l], ffn_conv_b[l], ffn_w_out[l])
        xl = xl + ml[5] * conv_ffn(hl, ffn_w_in[l], ffn_conv_w[l], ffn_conv_b[l], ffn_w_out[l])
    y_prompt = rmsnorm(xc, norm_final)
    y_sample = rmsnorm(xl, norm_final)
    return (y_prompt, y_sample, jnp.stack(new_sf, axis=1), jnp.stack(new_sb, axis=1),
            jnp.stack(new_k, axis=1), jnp.stack(new_v, axis=1))


_drawn_inputs = setup_inputs


def setup_inputs(seed=0):
    import zlib

    import numpy as np

    out = dict(_drawn_inputs(seed))
    spreads = {}
    factors = {'norm_ffn': 3.493,
     'attn_sink': 28.219,
     'ffn_conv_b': 4.068,
     'norm_final': 8.585,
     'cache_attn_k': 8.0,
     'cache_attn_v': 7.752}
    for name, (base, spread) in spreads.items():
        noise = np.random.default_rng([zlib.crc32(name.encode()), seed]).standard_normal(out[name].shape)
        drawn = base * np.exp(spread * noise) if base else spread * noise
        out[name] = __import__('jax').numpy.asarray(drawn.astype(out[name].dtype))
    for name, factor in factors.items():
        out[name] = (out[name] * factor).astype(out[name].dtype)
    return out
```

```python
from contextlib import ExitStack

import concourse.bass as bass
from concourse import mybir

F32 = mybir.dt.float32
F32R = mybir.dt.float32r
BF16 = mybir.dt.bfloat16
ALU = mybir.AluOpType
ACT = mybir.ActivationFunctionType
AX = mybir.AxisListType

P = 128
D = 1024
KT = D // P
NCTX, NLAT = 128, 512
T = NCTX + NLAT
TT = T // P
HALF = T // 2
CUT = HALF - NCTX
HEADS, DK, DV = 4, 256, 512
QH, KVH, HD = 16, 4, 64
G = QH // KVH
FF = 2816
FT = FF // P
GROUPS = (8, 8, 6)
EPS = 1e-6
NEG = -1e30
RAW = 4
RING = 2
CH = 8 * P
PAD = T + 3
CONV = T + 1
LAT_AT = NCTX + 1

C_ID, C_ONE, C_SEL, C_ZF, C_ZB = 0, 128, 256, 258, 259
C_W = 260
V_C, V_ADAB, V_NORM, V_DEC, V_SINK = 0, 16, 112, 152, 160
V_CONV = 176
V_W = V_CONV + 2 * 2 * FT * 4


class Body:

    def __init__(self, c0, m0, kinds):
        self.c0, self.m0, self.kinds = c0, m0, kinds
        self.raw, self.mains = len(kinds), kinds.count("m")
        self.at = [k for k, x in enumerate(kinds) if x == "m"] + [len(kinds), len(kinds) + 1]
        self.ada = [k for k, x in enumerate(kinds) if x == "a"]

    def chunk(self, k, i):
        c = self.c0 + k
        return c % RAW, c // RAW + 1 + (self.raw // RAW) * i

    def split(self, j, i):
        m = self.m0 + j
        return m % RING, m // RING + 1 + (self.mains // RING) * i

    def done(self, j, i):
        return self.m0 + j + 1 + self.mains * i


def plan():
    seg = {}
    seg["ret0"] = Body(16, 0, "mmmm" + "a" * 8 + "m" * 12)
    seg["ret"] = Body(40 - 28, 16 - 20, "mmmmmmmm" + "a" * 8 + "m" * 12)
    seg["wo3"] = Body(124, 76, "mmmm")
    c, m = 128, 80
    for layer in range(2):
        for g, tiles in enumerate(GROUPS):
            kinds = "mmmm"
            if layer == 0 and g == 0:
                kinds = "mm" + "a" * 8 + "mm"
            if layer == 0 and g == 1:
                kinds = "mm" + "a" * 8 + "mmmmmm"
            b = Body(c, m, kinds)
            seg["in", layer, g] = b
            turns = 2 * tiles // b.mains
            c, m = c + turns * b.raw, m + turns * b.mains
            seg["out", layer, g] = Body(c, m, "m" * tiles)
            c, m = c + tiles, m + tiles
        if layer == 0:
            seg["att"] = Body(c, m, "m" * 12)
            seg["att_o"] = Body(c + 12, m + 12, "m" * 8)
            c, m = c + 20, m + 20
    return seg, c, m


SEG, CHUNKS, MAINS = plan()
Y_ORDER = (0, 3, 2, 4, 1)
AT_LOADS = 3 + KVH
UNITS = (TT) * KVH


def band(n):
    return max(n - 1, 0), min(n + 2, NLAT // P)


def key_blocks(n):
    return [0] if n == 4 else [None] + [1 + b for b in range(*band(n))]


def tok_of(n):
    return slice(0, NCTX) if n == 4 else slice(NCTX + n * P, NCTX + (n + 1) * P)


PT_AT = [sum(len(key_blocks(x // KVH)) for x in range(u)) for u in range(UNITS)]


def over(ap, n):
    return ap.unsqueeze(1).to_broadcast([ap.shape[0], n, ap.shape[1]])


def build(nc, dr):
    with ExitStack() as ctx:
        def sb(name, shape, dt=F32, where=ctx):
            return where.enter_context(nc.sbuf_tensor(name, shape, dt))

        def sem(name):
            return ctx.enter_context(nc.semaphore(name))

        ps = ctx.enter_context(nc.psum_tensor("ps", [P, 8, 512], F32))

        xT = sb("xT", [P, KT, T])
        raw = sb("raw", [P, RAW, CH])
        w_h, w_l = sb("w_h", [P, RING, CH], F32R), sb("w_l", [P, RING, CH], F32R)
        h_h, h_l = sb("h_h", [P, KT, T], F32R), sb("h_l", [P, KT, T], F32R)
        cst = sb("cst", [P, C_W])
        vec = sb("vec", [P, V_W])
        mods = sb("mods", [P, 2, 48, 2])
        mod_a = sb("mod_a", [P, KT, 2])
        csil = sb("csil", [P, KT, 32])
        ada_o = sb("ada_o", [P, 2, 512])
        small = sb("small", [P, 96])
        front = sb("front", [P, 8 * T])
        ident, ones, sel = cst[:, C_ID:C_ID + P], cst[:, C_ONE:C_ONE + P], cst[:, C_SEL:C_SEL + 2]
        eps = small[:, 95:96]
        conv_w = vec[:, V_CONV:V_W].rearrange("p (l t k) -> p l t k", l=2, k=4)
        ada_b = vec[:, V_ADAB:V_ADAB + 96].rearrange("p (l t) -> p l t", l=2)
        norm_g = vec[:, V_NORM:V_NORM + 40].rearrange("p (n t) -> p n t", n=5)
        sq = front[:, 0:2 * T].rearrange("p (b t) -> p b t", b=2)
        root = front[:, 2 * T:3 * T]
        rstd = front[:, 3 * T:4 * T]
        xn = front[:, 4 * T:6 * T].rearrange("p (b t) -> p b t", b=2)
        hf = front[:, 6 * T:8 * T].rearrange("p (b t) -> p b t", b=2)

        with ExitStack() as ret:
            v = front[:, 0:TT * 512].rearrange("p (t d) -> p t d", t=TT)
            gf = front[:, TT * 512:2 * TT * 512].rearrange("p (t d) -> p t d", t=TT)
            gb = sb("gb", [P, TT, 512], F32, ret)
            qT, kT = sb("qT", [P, 2, T], F32, ret), sb("kT", [P, 2, T], F32, ret)
            qf = sb("qf", [P, 2, NLAT], F32, ret)
            S = sb("S", [P, 2, 2, DV], F32, ret)
            kz = sb("kz", [P, 2, 4, DK], F32, ret)
            rope_t = sb("rope_t", [P, 2, NLAT], F32, ret)
            dm = sb("dm", [P, 2, HEADS, P], F32, ret)
            xi = sb("xi", [P, 2, HEADS, P], F32, ret)
            st_out = sb("st_out", [P, 2, 2, DV], F32, ret)
            junk = sb("junk", [P, 512], F32, ret)
            y_h, y_l = sb("y_h", [P, 4, T], F32R, ret), sb("y_l", [P, 4, T], F32R, ret)
        with ExitStack() as ffn:
            ca = sb("ca", [P, 2, 2, PAD + 1], F32, ffn)
            cc = sb("cc", [P, 2, 2, CONV + 1], F32, ffn)
            sg = sb("sg", [P, 2, CONV + 1], F32, ffn)
            md = sb("md", [P, 2, T], F32, ffn)
            m_h, m_l = sb("m_h", [P, 8, T], F32R, ffn), sb("m_l", [P, 8, T], F32R, ffn)
        with ExitStack() as att:
            aq = sb("aq", [P, KT, T], F32, att)
            ak = sb("ak", [P, KVH, T], F32, att)
            ck = sb("ck", [P, KVH, NCTX], F32, att)
            av = sb("av", [P, TT, KVH * HD], F32, att)
            cv = sb("cv", [P, KVH * HD], F32, att)
            rope_a = sb("rope_a", [P, 2, NLAT], F32, att)
            maskf = sb("maskf", [P, 2, P], F32, att)
            maskb = sb("maskb", [P, 2, P], BF16, att)
            identb = sb("identb", [P, P], BF16, att)
            pr = sb("pr", [P, 2, G, 512], F32, att)
            pT = sb("pT", [P, 2, 4, 512], F32, att)
        lat_in = front[:, 0:4 * NLAT].rearrange("p (b t) -> p b t", b=4)
        swapped = front[:, 4 * NLAT:5 * NLAT]
        r1, r2 = front[:, 5 * NLAT:6 * NLAT], front[:, 6 * NLAT:7 * NLAT]

        iota = st_out[:, 0, 0, 0:2 * P].rearrange("p (d i) -> p d i", d=2)
        tri = st_out[:, 0, 1, 0:2 * P].rearrange("p (d i) -> p d i", d=2)

        raw_landed = [sem(f"raw_landed{s}") for s in range(RAW)]
        raw_used = [sem(f"raw_used{s}") for s in range(RAW)]
        hi_ready = [sem(f"hi_ready{s}") for s in range(RING)]
        chunk_done = sem("chunk_done")
        const_in, vec_in, x_in = sem("const_in"), sem("vec_in"), sem("x_in")
        eps_set = sem("eps_set")
        csil_zero, csil_ready = sem("csil_zero"), sem("csil_ready")
        ada_copied, ada_turned, mods_done = sem("ada_copied"), sem("ada_turned"), sem("mods_done")
        a_ready = sem("a_ready")
        sq_done, sum_done, root_done = sem("sq_done"), sem("sum_done"), sem("root_done")
        hf_done, hhi_done, hlo_done = sem("hf_done"), sem("hhi_done"), sem("hlo_done")
        out_done = sem("out_done")
        res_done = sem("res_done")
        dec_in, dec_abs, dec_e, dec_w, dec_ln, dec_lg = (sem(f"dec_{n}") for n in
                                                         ("in", "abs", "e", "w", "ln", "lg"))
        dec_exp, dec_ready = sem("dec_exp"), sem("dec_ready")
        rope_in = sem("rope_in")
        qk_evac, rope_done, tile_done, tok_evac = (sem(n) for n in ("qk_evac", "rope_done", "tile_done", "tok_evac"))
        scores_read = sem("scores_read")
        scores_done, sT_done, kz_done, S_in = (sem(n) for n in ("scores_done", "sT_done", "kz_done", "S_in"))
        o_done, u_done, S_upd, st_copied, st_stored = (sem(n) for n in
                                                       ("o_done", "u_done", "S_upd", "st_copied", "st_stored"))
        ss_done, rms_done, o_evac, y_done = (sem(n) for n in ("ss_done", "rms_done", "o_evac", "y_done"))
        yT_done, yhi_done, ylo_done = sem("yT_done"), sem("yhi_done"), sem("ylo_done")
        a_evac = [sem(f"a_evac{l}") for l in range(2)]
        conv_done = [sem(f"conv_done{l}") for l in range(2)]
        silu_done = [sem(f"silu_done{l}") for l in range(2)]
        md_done = [sem(f"md_done{l}") for l in range(2)]
        mhi_done = [sem(f"mhi_done{l}") for l in range(2)]
        mlo_done = [sem(f"mlo_done{l}") for l in range(2)]
        at_zero, at_in, at_bf, aqk_evac, arope_done = (sem(n) for n in
                                                       ("at_zero", "at_in", "at_bf", "aqk_evac", "arope_done"))
        atile_done, av_evac, as_done, am_done, ae_done, ap_done = (
            sem(n) for n in ("atile_done", "av_evac", "as_done", "am_done", "ae_done", "ap_done"))
        apt_done, apt_act, apt_dve, apv_done, aohi_done, aolo_done = (
            sem(n) for n in ("apt_done", "apt_act", "apt_dve", "apv_done", "aohi_done", "aolo_done"))
        y_scaled, y_stored, kv_stored = sem("y_scaled"), sem("y_stored"), sem("kv_stored")

        block = ctx.enter_context(nc.Block())

        def lo_hi(b):
            return slice(b * HALF, b * HALF + HALF)

        def wait_pt(eng, x):
            eng.wait_ge(apt_act if x % 2 == 0 else apt_dve, x // 2 + 1)

        def spans(b):
            if b == 0:
                return [(slice(0, NCTX), slice(0, NCTX), 1), (slice(NCTX, HALF), slice(NCTX, HALF), 0)]
            return [(slice(0, HALF), slice(HALF, T), 0)]

        @block.sync
        def _(sp):
            def load(c, i, turns):
                s = c % RAW
                if turns is not None:
                    sp.wait_ge(raw_used[s], turns)
                sp.dma_start(raw[:, s, :], dr["stream"][c + RAW * i]).then_inc(raw_landed[s], 16)

            for c in range(RAW):
                load(c, 0, None)
            with sp.Fori(1, CHUNKS // RAW) as i:
                for c in range(RAW):
                    load(c, i, i)
            sp.wait_ge(y_stored, 16 * KT)
            sp.wait_ge(st_stored, 32 * HEADS)
            sp.wait_ge(kv_stored, 16 * 5)

        @block.tensor
        def _(pe):
            def weights(b, j, i):
                s, n = b.split(j, i)
                pe.wait_ge(hi_ready[s], n)
                c, used = b.chunk(b.at[j], i)
                pe.wait_ge(raw_used[c], used)
                return s

            def feature_tile(b, j, i, banks, free):
                s = weights(b, j, i)
                for half in range(2):
                    free(half)
                    for k in range(KT):
                        wh, wl = (w[:, s, k * P:(k + 1) * P] for w in (w_h, w_l))
                        for n, (w, x) in enumerate(((wh, h_h), (wh, h_l), (wl, h_h))):
                            mm = nc.tensor.matmul(ps[:, banks + half, 0:HALF], w, x[:, k, lo_hi(half)],
                                                  start=(k == 0 and n == 0), stop=(k == KT - 1 and n == 2))
                mm.then_inc(chunk_done, 1)

            def token_chunk(b, j, i, kc, ks, n_cols, bank, free):
                s = weights(b, j, i)
                last = kc == KT // ks - 1
                for t in range(TT):
                    if kc == 0:
                        free(t)
                    for kk in range(ks):
                        k = kc * ks + kk
                        wh, wl = (w[:, s, kk * n_cols:(kk + 1) * n_cols] for w in (w_h, w_l))
                        for n, (x, w) in enumerate(((h_h, wh), (h_h, wl), (h_l, wh))):
                            mm = nc.tensor.matmul(ps[:, bank(t), 0:n_cols], x[:, k, t * P:(t + 1) * P], w,
                                                  start=(k == 0 and n == 0), stop=(k == KT - 1 and n == 2))
                    if t == TT - 1:
                        mm.then_inc(chunk_done, 1)
                    elif last:
                        mm.then_inc(tile_done if n_cols == 512 else atile_done, 1)

            def out_proj(b, j0, i, tiles, xh, xl, ready, free):
                j = j0
                for mh in range(2):
                    for kc in range(tiles // 2):
                        s = weights(b, j, i)
                        ready(kc)
                        for bank in range(8):
                            mt, half = bank // 2, bank % 2
                            if kc == 0:
                                free(mh, bank)
                            for kk in range(2):
                                k = 2 * kc + kk
                                c = kk * 512 + mt * P
                                wh, wl = w_h[:, s, c:c + P], w_l[:, s, c:c + P]
                                for n, (w, x) in enumerate(((wh, xh), (wh, xl), (wl, xh))):
                                    mm = nc.tensor.matmul(ps[:, bank, 0:HALF], w, x[:, k, lo_hi(half)],
                                                          start=(k == 0 and n == 0),
                                                          stop=(k == tiles - 1 and n == 2))
                            if kc == tiles // 2 - 1 and bank < 7:
                                mm.then_inc(out_done, 1)
                        mm.then_inc(chunk_done, 1)
                        j += 1

            def ada_block(b, k0, i, par):
                for kc in range(4):
                    s, n = b.chunk(b.ada[k0 + kc], i)
                    pe.wait_ge(raw_landed[s], 16 * n)
                    for kk in range(2):
                        k = 2 * kc + kk
                        g = k % 4
                        mm = nc.tensor.matmul(ps[32 * g:32 * g + 32, 4 + par, :], csil[:, k, :],
                                              raw[:, s, kk * 512:(kk + 1) * 512], start=(k < 4), stop=(k >= 4))
                    mm.then_inc(raw_used[s], 1)

            def ada_turn(par, copied, free):
                pe.wait_ge(ada_copied, copied)
                if free is not None:
                    pe.wait_ge(mods_done, free)
                for f in range(4):
                    mm = nc.tensor.matmul(ps[:, 6 + par, 2 * f:2 * f + 2],
                                          ada_o[:, par, f * P:(f + 1) * P], sel, start=True, stop=True)
                mm.then_inc(ada_turned, 1)

            def norm_sum(n, free):
                free()
                for k in range(KT):
                    pe.wait_ge(sq_done, KT * n + k + 1)
                    for half in range(2):
                        mm = nc.tensor.matmul(ps[:, half, 0:HALF], ones, sq[:, k % 2, lo_hi(half)],
                                              start=(k == 0), stop=(k == KT - 1))
                    mm.then_inc(sum_done, 1)

            def wait_h(n):
                pe.wait_ge(hlo_done, KT * (n + 1))
                pe.wait_ge(root_done, n + 1)

            pe.wait_ge(const_in, 16)
            pe.wait_ge(csil_ready, 1)
            norm_sum(0, lambda: None)
            first = Body(0, 0, "a" * 16)
            for blk in range(4):
                if blk >= 2:
                    pe.wait_ge(ada_copied, blk - 1)
                ada_block(first, 4 * blk, 0, blk % 2)
                ada_turn(blk % 2, blk + 1, blk - 1 if blk >= 2 else None)

            def head(b, h, first_head):
                for j in range(4):
                    def free(half, j=j):
                        if half:
                            return
                        if j >= 2:
                            pe.wait_ge(qk_evac, 4 * h + j - 1)
                        elif not first_head:
                            pe.wait_ge(S_upd, 6 * h)
                    feature_tile(b, j, h, 2 * (j % 2), free)
                j = 4
                if not first_head:
                    turn_y(h - 1)
                    out_proj(b, 4, h, 4, y_h, y_l, lambda kc: None, free_out(h - 1, h))
                    j = 8
                if not first_head:
                    pe.wait_ge(res_done, 16 * h)
                for blk in range(2):
                    pe.wait_ge(ada_copied, 4 + 2 * h + blk - 1)
                    ada_block(b, 4 * blk, h, blk)
                pe.wait_ge(qk_evac, 4 * h + 4)
                for proj in range(3):
                    for kc in range(4):
                        def free(t, proj=proj):
                            if proj == 0:
                                if t == 4:
                                    pe.wait_ge(ada_copied, 4 + 2 * h + 1)
                            else:
                                pe.wait_ge(tok_evac, 15 * h + 5 * (proj - 1) + t + 1)
                                if t == 3 and proj == 1:
                                    pe.wait_ge(scores_read, h + 1)
                                if t == 4 and proj == 1:
                                    pe.wait_ge(kz_done, h + 1)
                        token_chunk(b, j, h, kc, 2, 512, lambda t: t, free)
                        j += 1
                        if proj == 0 and kc == 0:
                            for blk in range(2):
                                ada_turn(blk, 4 + 2 * h + blk + 1, 4 + 2 * h + blk - 1)
                    if proj == 0:
                        scores(h)
                steps(h)

            def scores(h):
                pe.wait_ge(rope_done, 2 * h + 2)
                pe.wait_ge(mods_done, 4 + 2 * h + 2)
                pe.wait_ge(tok_evac, 15 * h + 5)
                for c in range(TT):
                    for t in range(2):
                        tok = slice(c * P, (c + 1) * P)
                        out = ps[:, 3, 0:P] if c == 0 else ps[:, 5, (c - 1) * P:c * P]
                        nc.tensor.matmul(out, kT[:, t, tok], qT[:, t, tok], start=(t == 0), stop=(t == 1))
                for c in range(TT):
                    for t in range(2):
                        bank, col = ((6, P), (7, 0), (7, DK), (4, 0), (4, DK))[c]
                        mm = nc.tensor.transpose(ps[:, bank, col + t * P:col + (t + 1) * P],
                                                 kT[:, t, c * P:(c + 1) * P], ident)
                mm.then_inc(scores_done, 1)

            def steps(h):
                pe.wait_ge(sT_done, h + 1)
                pe.wait_ge(tok_evac, 15 * h + 15)
                pe.wait_ge(S_in, 16 * h + 16)
                for d in range(2):
                    nc.tensor.matmul(ps[:, 6 + d, :], kT[:, d, 0:P], v[:, 0, :],
                                     start=True, stop=True).then_inc(o_done, 1)
                for d in range(2):
                    for t in range(2):
                        mm = nc.tensor.matmul(ps[:, 2 * d + t, :], kz[:, d, 0, t * P:(t + 1) * P], v[:, 0, :],
                                              start=True, stop=True)
                    mm.then_inc(u_done, 1)
                for s in range(4):
                    for d in range(2):
                        c = s if d == 0 else 3 - s
                        q = qf if d == 0 else qT[:, :, NCTX:T]
                        pe.wait_ge(o_evac, 10 * h + 2 * s + d + 1)
                        nc.tensor.matmul(ps[:, 6 + d, :], kT[:, d, (c + 1) * P:(c + 2) * P], v[:, c + 1, :],
                                         start=True, stop=False)
                        if s >= 1:
                            pe.wait_ge(S_upd, 6 * h + 2 * (s - 1) + d + 1)
                        for t in range(2):
                            mm = nc.tensor.matmul(ps[:, 6 + d, :], q[:, t, c * P:(c + 1) * P], S[:, d, t, :],
                                                  start=False, stop=(t == 1))
                        mm.then_inc(o_done, 1)
                        if s == 3:
                            continue
                        if s == 0:
                            pe.wait_ge(st_copied, 2 * h + d + 1)
                        slot = c + 1 if d == 0 else c
                        for t in range(2):
                            mm = nc.tensor.matmul(ps[:, 2 * d + t, :], kz[:, d, slot, t * P:(t + 1) * P],
                                                  v[:, c + 1, :], start=True, stop=True)
                        mm.then_inc(u_done, 1)

            def turn_y(h):
                for n, t in enumerate(Y_ORDER):
                    pe.wait_ge(y_done, TT * h + n + 1)
                    if n >= 3:
                        pe.wait_ge(ylo_done, TT * h + n - 2)
                    elif n >= 1:
                        pe.wait_ge(o_evac, 10 * h + 8 + n)
                    for k in range(4):
                        mm = nc.tensor.transpose(ps[:, 5 + n % 3, k * P:(k + 1) * P],
                                                 gf[:, t, k * P:(k + 1) * P], ident)
                    mm.then_inc(yT_done, 1)
                pe.wait_ge(ylo_done, TT * h + TT)

            def free_out(o, h):
                def free(mh, bank):
                    if mh == 1:
                        pe.wait_ge(res_done, 16 * o + bank + 1)
                    elif bank == 0 and h is not None:
                        pe.wait_ge(qk_evac, 4 * h + 4)
                return free

            wait_h(0)
            head(SEG["ret0"], 0, True)
            with pe.Fori(1, HEADS) as h:
                head(SEG["ret"], h, False)
            turn_y(HEADS - 1)
            out_proj(SEG["wo3"], 0, 0, 4, y_h, y_l, lambda kc: None, free_out(3, None))

            def ffn_phase(l, o0):
                tiles0 = 0
                for g, tiles in enumerate(GROUPS):
                    b = SEG["in", l, g]
                    pairs = b.mains // 2

                    def pair_group(i, l=l, g=g, b=b, pairs=pairs, tiles0=tiles0):
                        for q in range(pairs):
                            n = tiles0 + q
                            for w in range(2):
                                def free(half, w=w, n=n):
                                    if half == 0:
                                        pe.wait_ge(a_evac[l], 2 * n + w + 1 + 2 * pairs * i)
                                feature_tile(b, 2 * q + w, i, 2 * w, free)
                                if b.ada and q == 1 and w == 0:
                                    for blk in range(2):
                                        n_blk = 12 + 8 * g + blk
                                        ada_turn(blk, n_blk + 1 + 2 * i, n_blk - 1 + 2 * i)
                            if b.ada and q == 0:
                                for blk in range(2):
                                    pe.wait_ge(ada_copied, 12 + 8 * g + blk - 1 + 2 * i)
                                    ada_block(b, 4 * blk, i, blk)

                    with pe.Fori(0, tiles // pairs) as i:
                        pair_group(i)
                    if b.ada:
                        pe.wait_ge(mods_done, 12 + 8 * g + 2 * (tiles // pairs))
                    done = tiles0 + tiles

                    def ready(kc, l=l, done=done, tiles=tiles):
                        pe.wait_ge(mlo_done[l], done - tiles + 2 * kc + 2)

                    def free(mh, bank, l=l, done=done, o=o0 + g):
                        if mh == 1:
                            pe.wait_ge(res_done, 16 * o + bank + 1)
                        elif bank == 0:
                            pe.wait_ge(a_evac[l], 2 + 2 * done)
                    out_proj(SEG["out", l, g], 0, 0, tiles, m_h, m_l, ready, free)
                    tiles0 = done
                    if g < 2:
                        pe.wait_ge(res_done, 16 * (o0 + g) + (16 if SEG["in", l, g + 1].ada else 12))

            def free_norm(o):
                return lambda: pe.wait_ge(res_done, 16 * o + 10)

            norm_sum(1, free_norm(3))
            wait_h(1)
            pe.wait_ge(res_done, 16 * 4)
            ffn_phase(0, 4)
            norm_sum(2, free_norm(6))
            wait_h(2)
            pe.wait_ge(res_done, 16 * 7)

            b = SEG["att"]
            for j in range(10):
                def free(half, j=j):
                    if half == 0 and j >= 2:
                        pe.wait_ge(aqk_evac, j - 1)
                feature_tile(b, j, 0, 2 * (j % 2), free)
            for kc in range(2):
                def free(t):
                    if t == 4:
                        pe.wait_ge(aqk_evac, 9)
                token_chunk(b, 10 + kc, 0, kc, 4, KVH * HD, lambda t: (4 + t) % 8, free)
            pe.wait_ge(aqk_evac, 10)
            pe.wait_ge(av_evac, TT)
            pe.wait_ge(arope_done, 10)
            pe.wait_ge(at_in, 16 * AT_LOADS)
            pe.wait_ge(at_bf, 1)
            pt_n = 0

            def unit_scores(u):
                n, kv = divmod(u, KVH)
                if u >= 1:
                    pe.wait_ge(ae_done, u)
                for g in range(G):
                    q = aq[:, (kv // 2) * G + g, tok_of(n)]
                    if n == 4:
                        mm = nc.tensor.matmul(ps[:, g, 0:P], q, ak[:, kv, 0:NCTX], start=True, stop=True)
                        continue
                    nc.tensor.matmul(ps[:, g, 0:P], q, ck[:, kv, :], start=True, stop=True)
                    lo, hi = band(n)
                    nc.tensor.matmul(ps[:, g, P:P * (1 + hi - lo)], q, ak[:, kv, NCTX + lo * P:NCTX + hi * P],
                                     start=True, stop=False)
                    if n > lo:
                        mm = nc.tensor.matmul(ps[:, g, P:2 * P], identb[:], maskb[:, 0, :], start=False, stop=(n + 1 >= hi))
                    if n + 1 < hi:
                        mm = nc.tensor.matmul(ps[:, g, P * (hi - lo):P * (hi - lo + 1)], identb[:], maskb[:, 1, :],
                                              start=False, stop=True)
                mm.then_inc(as_done, 1)

            def unit_values(u, pt_n):
                n, kv = divmod(u, KVH)
                kbs = key_blocks(n)
                pe.wait_ge(ap_done, u + 1)
                for kb in range(len(kbs)):
                    x = pt_n + kb
                    if x >= 2:
                        wait_pt(pe, x - 2)
                    for g in range(G):
                        mm = nc.tensor.transpose(ps[:, 4 + x % 2, g * P:(g + 1) * P],
                                                 pr[:, u % 2, g, kb * P:(kb + 1) * P], ident)
                    mm.then_inc(apt_done, 1)
                if kv % 2 == 0 and u >= 4:
                    pe.wait_ge(aolo_done, (u - 4) // 2 + 1)
                for kb, src in enumerate(kbs):
                    wait_pt(pe, pt_n + kb)
                    val = cv if src is None else av[:, src, :]
                    mm = nc.tensor.matmul(ps[64 * (kv % 2):64 * (kv % 2) + 64, 6 + (u // 2) % 2, :],
                                          val[:, kv * HD:(kv + 1) * HD], pT[:, u % 2, kb, :],
                                          start=(kb == 0), stop=(kb == len(kbs) - 1))
                mm.then_inc(apv_done, 1)

            unit_scores(0)
            for u in range(UNITS):
                if u + 1 < UNITS:
                    unit_scores(u + 1)
                unit_values(u, PT_AT[u])
            pe.wait_ge(aolo_done, UNITS // 2)
            pe.wait_ge(ae_done, UNITS)

            def free(mh, bank):
                if mh == 1:
                    pe.wait_ge(res_done, 16 * 7 + bank + 1)
            out_proj(SEG["att_o"], 0, 0, KT, h_h, h_l, lambda kc: None, free)
            norm_sum(3, free_norm(7))
            wait_h(3)
            pe.wait_ge(res_done, 16 * 8)
            ffn_phase(1, 8)
            norm_sum(4, free_norm(10))

        @block.scalar
        def _(act):
            def hi(b, j, i):
                if b is None:
                    return
                s, landed = b.chunk(b.at[j], i)
                r, n = b.split(j, i)
                act.wait_ge(raw_landed[s], 16 * landed)
                if not (b.m0 + j < RING and isinstance(i, int)):
                    act.wait_ge(chunk_done, b.done(j, i) - RING)
                nc.scalar.copy(w_h[:, r, :], raw[:, s, :]).then_inc(hi_ready[r], 1)

            act.dma_start(vec[:], dr["vec"]).then_inc(vec_in, 16)
            act.dma_start(xT[:], dr["x"]).then_inc(x_in, 16)
            act.dma_start(cst[:], dr["cst"]).then_inc(const_in, 16)
            act.dma_start(dm[:], dr["diff"]).then_inc(dec_in, 16)
            act.dma_start(iota, dr["iota"]).then_inc(dec_in, 16)
            act.dma_start(tri, dr["tri"]).then_inc(dec_in, 16)
            act.dma_start(rope_t[:], dr["rope_t"]).then_inc(rope_in, 16)

            act.wait_ge(vec_in, 16)
            act.wait_ge(csil_zero, 1)
            cvec = vec[:, V_C:V_C + 16].rearrange("p (k s) -> p k s", s=2)
            nc.scalar.activation(csil[:, :, 0:2], cvec, ACT.Silu).then_inc(csil_ready, 1)

            def norm_act(n, ready):
                for k in range(KT):
                    ready(k)
                    if KT * n + k >= 2:
                        act.wait_ge(sum_done, KT * n + k - 1)
                    nc.scalar.activation(sq[:, k % 2, :], xT[:, k, :], ACT.Square).then_inc(sq_done, 1)
                act.wait_ge(sum_done, KT * n + KT)
                nc.scalar.activation(root.rearrange("p (b t) -> p b t", b=2), ps[:, 0:2, 0:HALF], ACT.Sqrt,
                                     bias=eps, scale=1.0 / D).then_inc(root_done, 1)

            def norm_hi(n):
                for k in range(KT):
                    act.wait_ge(hf_done, KT * n + k + 1)
                    nc.scalar.copy(h_h[:, k, :], hf[:, k % 2, :]).then_inc(hhi_done, 1)

            act.wait_ge(x_in, 16)
            act.wait_ge(eps_set, 1)
            norm_act(0, lambda k: None)

            act.wait_ge(dec_abs, 1)
            nc.scalar.activation(small[:, 8:16], small[:, 0:8], ACT.Exp, scale=-1.0).then_inc(dec_e, 1)
            act.wait_ge(dec_w, 1)
            nc.scalar.activation(small[:, 24:32], small[:, 16:24], ACT.Ln).then_inc(dec_ln, 1)
            act.wait_ge(dec_lg, 1)
            act.wait_ge(dec_in, 48)
            act.wait_ge(const_in, 16)
            for d in range(2):
                for h in range(HEADS):
                    lg = small[:, 40 + 4 * d + h:41 + 4 * d + h]
                    nc.scalar.activation(dm[:, d, h, :], dm[:, d, h, :], ACT.Exp, scale=lg)
                    nc.scalar.activation(xi[:, d, h, :], iota[:, d, :], ACT.Exp, scale=lg)
                    nc.scalar.activation(small[:, 48 + 4 * d + h:49 + 4 * d + h],
                                         cst[:, C_ZF + d:C_ZF + d + 1], ACT.Exp, scale=lg)
            nc.scalar.activation(small[:, 56:64], small[:, 40:48], ACT.Exp, scale=float(P)).then_inc(dec_exp, 1)

            norm_hi(0)
            b0 = SEG["ret0"]
            hi(b0, 0, 0)
            hi(b0, 1, 0)
            zeta = small[:, 48:56].rearrange("p (d h) -> p d h", d=2)

            def head(b, h, first_head):
                for j in range(4):
                    act.wait_ge(chunk_done, b.done(j, h))
                    hi(b, j + 2, h)
                    bank, scale = 2 * (j % 2), 1.0 if j < 2 else DK ** -0.5
                    ctx_to = (qT if j < 2 else kT)[:, j % 2, 0:NCTX]
                    lat = front[:, j * NLAT:(j + 1) * NLAT]
                    nc.scalar.activation(ctx_to, ps[:, bank, 0:NCTX], ACT.Copy, scale=scale)
                    nc.scalar.activation(lat[:, 0:CUT], ps[:, bank, NCTX:HALF], ACT.Copy, scale=scale)
                    nc.scalar.activation(lat[:, CUT:NLAT], ps[:, bank + 1, 0:HALF], ACT.Copy,
                                         scale=scale).then_inc(qk_evac, 1)
                    if j == 0:
                        act.dma_start(S[:], dr["state"][h]).then_inc(S_in, 16)
                j = 4
                if not first_head:
                    turn_y(h - 1)
                    for k in range(4):
                        hi(b, 4 + k + 2, h)
                    j = 8
                for proj in range(3):
                    for kc in range(3):
                        hi(b, j + kc + 2, h)
                    for t in range(TT):
                        if t == TT - 1:
                            act.wait_ge(chunk_done, b.done(j + 3, h))
                        else:
                            act.wait_ge(tile_done, 12 * h + 4 * proj + t + 1)
                        if proj == 0:
                            if t == 0:
                                act.wait_ge(rope_done, 2 * h + 2)
                            op = nc.scalar.copy(v[:, t, :], ps[:, t, :])
                        else:
                            op = nc.scalar.activation((gf, gb)[proj - 1][:, t, :], ps[:, t, :], ACT.Silu)
                        op.then_inc(tok_evac, 1)
                    hi(b, j + 3 + 2, h)
                    j += 4
                    if proj == 0:
                        act.wait_ge(scores_done, h + 1)
                        if first_head:
                            act.wait_ge(dec_ready, 1)
                        zf, zb = zeta[:, 0, bass.ds(h, 1)], zeta[:, 1, bass.ds(h, 1)]
                        pair = lambda bank: ps[:, bank, :].rearrange("p (c d) -> p c d", c=2)
                        nc.scalar.activation(kz[:, 0, 0, :], ps[:, 6, P:P + DK], ACT.Copy, scale=zf)
                        nc.scalar.activation(kz[:, 1, 0, :], ps[:, 6, P:P + DK], ACT.Copy, scale=zb)
                        nc.scalar.activation(kz[:, 0, 1:3, :], pair(7), ACT.Copy, scale=zf)
                        nc.scalar.activation(kz[:, 1, 1, :], ps[:, 7, DK:2 * DK], ACT.Copy, scale=zb)
                        nc.scalar.activation(kz[:, 0, 3, :], ps[:, 4, 0:DK], ACT.Copy, scale=zf)
                        nc.scalar.activation(kz[:, 1, 2:4, :], pair(4), ACT.Copy, scale=zb).then_inc(kz_done, 1)
                for n in range(10):
                    act.drain()
                    act.wait_ge(o_done, 10 * h + n + 1)
                    nc.scalar.activation(junk[:], ps[:, 6 + n % 2, :], ACT.Square,
                                         accum_out=small[:, 64 + n:65 + n]).then_inc(ss_done, 1)
                    if n == 1:
                        if not first_head:
                            act.wait_ge(st_stored, 32 * h)
                        for d in range(2):
                            act.wait_ge(u_done, 8 * h + d + 1)
                            nc.scalar.copy(st_out[:, d], ps[:, 2 * d:2 * d + 2, :]).then_inc(st_copied, 1)
                        for d in range(2):
                            act.wait_ge(st_copied, 2 * h + d + 1)
                            act.dma_start(dr["new_state"][d, h], st_out[:, d]).then_inc(st_stored, 16)

            def turn_y(h):
                for n, t in enumerate(Y_ORDER):
                    act.wait_ge(yT_done, TT * h + n + 1)
                    nc.scalar.copy(y_h[:, :, t * P:(t + 1) * P],
                                   ps[:, 5 + n % 3, :].rearrange("p (k q) -> p k q", k=4)).then_inc(yhi_done, 1)

            head(b0, 0, True)
            with act.Fori(1, HEADS) as h:
                head(SEG["ret"], h, False)
            turn_y(HEADS - 1)
            for j in range(4):
                hi(SEG["wo3"], j + 2, 0)

            def after_out(o):
                return lambda k: act.wait_ge(res_done, 16 * o + 2 * k + 2)

            def ffn_phase(l):
                tiles0 = 0
                for w in range(2):
                    nc.scalar.activation(small[:, 80 + w:81 + w], eps, ACT.Silu).then_inc(a_evac[l], 1)
                for g, tiles in enumerate(GROUPS):
                    b = SEG["in", l, g]
                    pairs = b.mains // 2
                    with act.Fori(0, tiles // pairs) as i:
                        for q in range(pairs):
                            n = tiles0 + q
                            par = q % 2
                            for w in range(2):
                                act.wait_ge(chunk_done, b.done(2 * q + w, i))
                                hi(b, 2 * q + w + 2, i)
                                act.wait_ge(conv_done[l], 2 * n + w + 1 + 2 * pairs * i)
                                a = ca[:, par, w]
                                nc.scalar.copy(a[:, 1:1 + NCTX], ps[:, 2 * w, 0:NCTX])
                                nc.scalar.copy(a[:, NCTX + 2:NCTX + 2 + CUT], ps[:, 2 * w, NCTX:HALF])
                                nc.scalar.copy(a[:, NCTX + 2 + CUT:NCTX + 2 + NLAT],
                                               ps[:, 2 * w + 1, 0:HALF]).then_inc(a_evac[l], 1)
                            act.wait_ge(conv_done[l], 4 + 2 * n + 2 + 2 * pairs * i)
                            nc.scalar.activation(sg[:, par, 0:CONV], cc[:, par, 1, 0:CONV],
                                                 ACT.Silu).then_inc(silu_done[l], 1)
                            act.wait_ge(md_done[l], n + 1 + pairs * i)
                            nc.scalar.copy(m_h[:, pairs * i + q, :], md[:, par, :]).then_inc(mhi_done[l], 1)
                    ob = SEG["out", l, g]
                    for j in range(tiles):
                        if ob.m0 + j + 2 < MAINS:
                            hi(ob, j + 2, 0)
                    tiles0 += tiles

            norm_act(1, after_out(3))
            norm_hi(1)
            ffn_phase(0)
            norm_act(2, after_out(6))
            act.wait_ge(at_zero, 1)
            act.dma_start(rope_a[:], dr["rope_a"]).then_inc(at_in, 16)
            act.dma_start(maskf[:], dr["mask"]).then_inc(at_in, 16)
            act.dma_start(cv[:], dr["cache_v"]).then_inc(at_in, 16)
            for kv in range(KVH):
                rows = slice(64 * (kv % 2), 64 * (kv % 2) + 64)
                act.dma_start(ck[rows, kv, :], dr["cache_k"][kv]).then_inc(at_in, 16)
            norm_hi(2)

            b = SEG["att"]
            for j in range(10):
                act.wait_ge(chunk_done, b.done(j, 0))
                hi(b, j + 2, 0)
                bank = 2 * (j % 2)
                if j >= 4:
                    act.wait_ge(arope_done, j - 3)
                if j == 0:
                    act.wait_ge(hlo_done, KT * 3)
                if j < 8:
                    nc.scalar.copy(aq[:, j, 0:NCTX], ps[:, bank, 0:NCTX])
                else:
                    for r in range(2):
                        rows = slice(64 * r, 64 * r + 64)
                        nc.scalar.copy(ak[rows, 2 * (j - 8) + r, 0:NCTX], ps[rows, bank, 0:NCTX])
                nc.scalar.copy(lat_in[:, j % 4, 0:CUT], ps[:, bank, NCTX:HALF])
                nc.scalar.copy(lat_in[:, j % 4, CUT:NLAT], ps[:, bank + 1, 0:HALF]).then_inc(aqk_evac, 1)
            hi(b, 12, 0)
            for t in range(TT):
                if t == TT - 1:
                    act.wait_ge(chunk_done, b.done(11, 0))
                else:
                    act.wait_ge(atile_done, t + 1)
                nc.scalar.copy(av[:, t, :], ps[:, (4 + t) % 8, 0:KVH * HD]).then_inc(av_evac, 1)
            hi(b, 13, 0)
            act.wait_ge(aqk_evac, 10)
            act.wait_ge(av_evac, 1)
            for kv in range(KVH):
                rows = slice(64 * (kv % 2), 64 * (kv % 2) + 64)
                act.dma_start(dr["new_k"][kv], ak[rows, kv, 0:NCTX]).then_inc(kv_stored, 16)
            act.dma_start(dr["new_v"], av[:, 0, :]).then_inc(kv_stored, 16)

            stat = small[:, 0:64].rearrange("p (a b) -> p a b", b=4)
            for u in range(UNITS + 1):
                if u < UNITS:
                    n, kv = divmod(u, KVH)
                    w = P * len(key_blocks(n))
                    st = 8 * (u % 2)
                    act.wait_ge(am_done, u + 1)
                    if u >= 2:
                        act.wait_ge(apv_done, u - 1)
                    for g in range(G):
                        nc.scalar.activation(pr[:, u % 2, g, 0:w], ps[:, g, 0:w], ACT.Exp, scale=HD ** -0.5,
                                             bias=stat[:, st + 1, g:g + 1], accum_out=stat[:, st + 3, g:g + 1])
                    nc.scalar.activation(stat[:, st + 4, :], stat[:, st + 2, :], ACT.Exp).then_inc(ae_done, 1)
                if u >= 1:
                    x0, n = PT_AT[u - 1], (u - 1) // KVH
                    for kb in range(len(key_blocks(n))):
                        if (x0 + kb) % 2 == 0:
                            act.wait_ge(apt_done, x0 + kb + 1)
                            if u >= 3 and kb < 2:
                                act.wait_ge(apv_done, u - 2)
                            nc.scalar.copy(pT[:, (u - 1) % 2, kb, :], ps[:, 4, :]).then_inc(apt_act, 1)
                    if (u - 1) % 2 == 1:
                        act.wait_ge(apv_done, u)
                        o = (u - 1) // 2
                        nc.scalar.copy(h_h[:, (o % 2) * G:(o % 2) * G + G, tok_of(n)],
                                       ps[:, 6 + o % 2, :].rearrange("p (g q) -> p g q", g=G)).then_inc(aohi_done, 1)
            for j in range(8):
                hi(SEG["att_o"], j + 2, 0)
            norm_act(3, after_out(7))
            norm_hi(3)
            ffn_phase(1)
            norm_act(4, after_out(10))
            for k in range(KT):
                act.wait_ge(hf_done, KT * 4 + k + 1)
                act.dma_start(dr["y"][k], aq[:, k, :]).then_inc(y_stored, 16)

        @block.gpsimd
        def _(pool):
            def lo(b, j, i):
                s, _ = b.chunk(b.at[j], i)
                r, n = b.split(j, i)
                pool.wait_ge(hi_ready[r], n)
                nc.gpsimd.tensor_tensor(w_l[:, r, :], raw[:, s, :], w_h[:, r, :].bitcast(F32),
                                        ALU.subtract).then_inc(raw_used[s], 1)

            nc.gpsimd.memset(small[:, 95:96], EPS).then_inc(eps_set, 1)
            nc.gpsimd.memset(csil[:], 0.0).then_inc(csil_zero, 1)
            nc.gpsimd.memset(small[:, 84:85], -0.5)
            nc.gpsimd.memset(small[:, 85:86], 1.0 / DV)
            pool.drain()

            def rms(h):
                for n in range(10):
                    pool.wait_ge(ss_done, 10 * h + n + 1)
                    out = small[:, 74 + n:75 + n]
                    nc.gpsimd.tensor_tensor(out, small[:, 64 + n:65 + n], small[:, 85:86], ALU.mult)
                    pool.drain()
                    nc.gpsimd.tensor_tensor(out, out, eps, ALU.add)
                    pool.drain()
                    nc.gpsimd.tensor_tensor(out, out, small[:, 84:85], ALU.pow).then_inc(rms_done, 1)

            for j in range(2):
                lo(SEG["ret0"], j, 0)
            for j in range(16):
                lo(SEG["ret0"], j + 2, 0)
            rms(0)
            with pool.Fori(1, HEADS) as h:
                for j in range(20):
                    lo(SEG["ret"], j + 2, h)
                rms(h)
            for j in range(4):
                lo(SEG["wo3"], j + 2, 0)
            for l in range(2):
                for g, tiles in enumerate(GROUPS):
                    b = SEG["in", l, g]
                    with pool.Fori(0, 2 * tiles // b.mains) as i:
                        for j in range(b.mains):
                            lo(b, j + 2, i)
                    ob = SEG["out", l, g]
                    for j in range(tiles):
                        if ob.m0 + j + 2 < MAINS:
                            lo(ob, j + 2, 0)
                if l == 0:
                    pool.wait_ge(res_done, 16 * 7)
                    nc.gpsimd.memset(ak[:], 0.0)
                    nc.gpsimd.memset(ck[:], 0.0)
                    pool.drain()
                    nc.gpsimd.memset(small[:, 94:95], 0.0).then_inc(at_zero, 1)
                    for j in range(12):
                        lo(SEG["att"], j + 2, 0)
                    for j in range(8):
                        lo(SEG["att_o"], j + 2, 0)

        @block.vector
        def _(dve):
            V = nc.vector

            def norm_dve(n, l, shift, scale):
                dve.wait_ge(root_done, n + 1)
                V.reciprocal(rstd, root)
                if n < 4:
                    for s in range(2):
                        V.scalar_tensor_tensor(out=mod_a[:, :, s], in0=mods[:, l, 8 * scale:8 * scale + 8, s], scalar=1.0,
                                               in1=norm_g[:, n, :], op0=ALU.add, op1=ALU.mult)
                dve.drain()
                if n == 4:
                    for k in range(KT):
                        V.scalar_tensor_tensor(out=aq[:, k, :], in0=xT[:, k, :], scalar=norm_g[:, 4, k:k + 1],
                                               in1=rstd, op0=ALU.mult, op1=ALU.mult).then_inc(hf_done, 1)
                    return
                for k in range(KT + 1):
                    if k < KT:
                        V.tensor_tensor(xn[:, k % 2, :], xT[:, k, :], rstd, ALU.mult)
                        dve.drain()
                        for s, tok in ((1, slice(0, NCTX)), (0, slice(NCTX, T))):
                            op = V.tensor_scalar(hf[:, k % 2, tok], xn[:, k % 2, tok], mod_a[:, k, s:s + 1],
                                                 mods[:, l, 8 * shift + k, s:s + 1], ALU.mult, ALU.add)
                        op.then_inc(hf_done, 1)
                    if k >= 1:
                        dve.wait_ge(hhi_done, KT * n + k)
                        V.tensor_tensor(h_l[:, k - 1, :], hf[:, (k - 1) % 2, :], h_h[:, k - 1, :].bitcast(F32),
                                        ALU.subtract).then_inc(hlo_done, 1)

            def ada_copy(b, k0, i, par, turned):
                s, n = b.chunk(b.ada[k0 + 3], i)
                dve.wait_ge(raw_used[s], n)
                if turned is not None:
                    dve.wait_ge(ada_turned, turned)
                V.tensor_copy(ada_o[:, par, :], ps[:, 4 + par, :]).then_inc(ada_copied, 1)

            def ada_mods(par, turned, l, blk):
                dve.wait_ge(ada_turned, turned)
                got = ps[:, 6 + par, 0:8].rearrange("p (f s) -> p f s", s=2)
                m5 = mods[:, l].rearrange("p (b f) s -> p b f s", f=4)
                b5 = ada_b[:, l].rearrange("p (b f) -> p b f", f=4)
                for s in range(2):
                    op = V.tensor_tensor(m5[:, blk, :, s], got[:, :, s], b5[:, blk, :], ALU.add)
                op.then_inc(mods_done, 1)

            def residual(o, b, j0, i, tiles, l, gate):
                for mh in range(2):
                    for bank in range(8):
                        if bank < 7:
                            dve.wait_ge(out_done, 14 * o + 7 * mh + bank + 1)
                        else:
                            dve.wait_ge(chunk_done, b.done(j0 + (mh + 1) * tiles // 2 - 1, i))
                        m = 4 * mh + bank // 2
                        for cols, tok, s in spans(bank % 2):
                            op = V.scalar_tensor_tensor(out=xT[:, m, tok], in0=ps[:, bank, cols],
                                                        scalar=mods[:, l, 8 * gate + m, s:s + 1],
                                                        in1=xT[:, m, tok], op0=ALU.mult, op1=ALU.add)
                        op.then_inc(res_done, 1)

            x, ab, e, w, ln, ra, lg = (vec[:, V_DEC:V_DEC + 8], *(small[:, 8 * n:8 * n + 8] for n in (0, 1, 2, 3, 4, 5)))
            t1, t2 = small[:, 64:72], small[:, 72:80]
            dve.wait_ge(vec_in, 16)
            V.tensor_scalar(t1, x, -1.0, None, ALU.mult)
            dve.drain()
            V.tensor_tensor(ab, x, t1, ALU.max).then_inc(dec_abs, 1)
            dve.wait_ge(dec_e, 1)
            V.tensor_scalar(w, e, 1.0, None, ALU.add).then_inc(dec_w, 1)
            dve.drain()
            V.tensor_scalar(t1, w, -1.0, 1e-30, ALU.add, ALU.max)
            dve.drain()
            V.reciprocal(t2, t1)
            dve.drain()
            V.tensor_tensor(ra, t2, e, ALU.mult)
            dve.drain()
            dve.wait_ge(dec_ln, 1)
            V.tensor_tensor(t1, ln, ra, ALU.mult)
            dve.drain()
            V.scalar_tensor_tensor(out=lg, in0=x, scalar=0.0, in1=t1, op0=ALU.min,
                                   op1=ALU.subtract).then_inc(dec_lg, 1)
            first = Body(0, 0, "a" * 16)
            for blk in range(4):
                ada_copy(first, 4 * blk, 0, blk % 2, blk - 1 if blk >= 2 else None)
                ada_mods(blk % 2, blk + 1, 0, blk)
            dve.drain()
            norm_dve(0, 0, 0, 1)
            dve.wait_ge(dec_exp, 1)
            for d in range(2):
                op = V.tensor_tensor(dm[:, d], dm[:, d], over(tri[:, d, :], HEADS), ALU.mult)
            op.then_inc(dec_ready, 1)
            gch = small[:, 56:64].rearrange("p (d h) -> p d h", d=2)

            def rope(dst, a, b, p1, p2):
                cos, sin = rope_t[:, 0], rope_t[:, 1]
                V.tensor_tensor(p1, a, cos, ALU.mult)
                V.tensor_tensor(p2, b, sin, ALU.mult)
                dve.drain()
                V.tensor_tensor(dst[:, 0, NCTX:T], p1, p2, ALU.subtract)
                dve.drain()
                V.tensor_tensor(p1, a, sin, ALU.mult)
                V.tensor_tensor(p2, b, cos, ALU.mult)
                dve.drain()
                V.tensor_tensor(dst[:, 1, NCTX:T], p1, p2, ALU.add).then_inc(rope_done, 1)
                dve.drain()

            def head(b, h, first_head):
                if first_head:
                    dve.wait_ge(rope_in, 16)
                lat = front[:, 0:4 * NLAT].rearrange("p (j t) -> p j t", j=4)
                for n, dst in enumerate((qT, kT)):
                    dve.wait_ge(qk_evac, 4 * h + 2 * n + 2)
                    rope(dst, lat[:, 2 * n], lat[:, 2 * n + 1], front[:, 4 * NLAT:5 * NLAT], gb[:, 0, :])
                if not first_head:
                    turn_y(h - 1)
                    residual(h - 1, b, 4, h, 4, 0, 2)
                for blk in range(2):
                    ada_copy(b, 4 * blk, h, blk, 4 + 2 * h + blk - 1)
                for blk in range(2):
                    ada_mods(blk, 4 + 2 * h + blk + 1, 0, 4 + 2 * h + blk)
                dve.wait_ge(scores_done, h + 1)
                for d in range(2):
                    V.tensor_tensor(kT[:, d, 0:P], ps[:, 3, 0:P], dm[:, d, h, :], ALU.mult)
                    op = V.tensor_tensor(kT[:, d, NCTX:T].rearrange("p (c i) -> p c i", c=4),
                                    ps[:, 5, :].rearrange("p (c i) -> p c i", c=4), over(dm[:, d, h, :], 4), ALU.mult)
                op.then_inc(scores_read, 1)
                for d in (0, 1):
                    for t in range(2):
                        src = qT[:, t, NCTX:T].rearrange("p (c i) -> p c i", c=4)
                        dst = src if d == 1 else qf[:, t, :].rearrange("p (c i) -> p c i", c=4)
                        op = V.tensor_tensor(dst, src, over(xi[:, d, h, :], 4), ALU.mult)
                    if d == 0:
                        dve.drain()
                op.then_inc(sT_done, 1)
                dve.wait_ge(tok_evac, 15 * h + 15)
                for n in range(10):
                    s, d = (n - 2) // 2, n % 2
                    t = 0 if n < 2 else 1 + (s if d == 0 else 3 - s)
                    if 2 <= n < 8:
                        dve.wait_ge(u_done, 8 * h + n + 1)
                        V.scalar_tensor_tensor(out=S[:, d], in0=S[:, d], scalar=gch[:, d, bass.ds(h, 1)],
                                               in1=ps[:, 2 * d:2 * d + 2, :], op0=ALU.mult,
                                               op1=ALU.add).then_inc(S_upd, 1)
                    dve.wait_ge(rms_done, 10 * h + n + 1)
                    g = (gf, gb)[d]
                    V.scalar_tensor_tensor(out=g[:, t, :], in0=ps[:, 6 + d, :], scalar=small[:, 74 + n:75 + n],
                                           in1=g[:, t, :], op0=ALU.mult, op1=ALU.mult).then_inc(o_evac, 1)
                    if n == 1 or n >= 6:
                        dve.drain()
                        V.tensor_tensor(gf[:, t, :], gf[:, t, :], gb[:, t, :], ALU.add).then_inc(y_done, 1)
                dve.drain()

            def turn_y(h):
                for n, t in enumerate(Y_ORDER):
                    dve.wait_ge(yhi_done, TT * h + n + 1)
                    cols = slice(t * P, (t + 1) * P)
                    V.tensor_tensor(y_l[:, :, cols], ps[:, 5 + n % 3, :].rearrange("p (k q) -> p k q", k=4),
                                    y_h[:, :, cols].bitcast(F32), ALU.subtract).then_inc(ylo_done, 1)

            head(SEG["ret0"], 0, True)
            with dve.Fori(1, HEADS) as h:
                head(SEG["ret"], h, False)
            turn_y(HEADS - 1)
            residual(3, SEG["wo3"], 0, 0, 4, 0, 2)

            def ffn_phase(l, o0):
                for par in range(2):
                    for w in range(2):
                        V.memset(ca[:, par, w], 0.0).then_inc(conv_done[l], 1)
                tiles0 = 0
                for g, tiles in enumerate(GROUPS):
                    b = SEG["in", l, g]
                    pairs = b.mains // 2
                    with dve.Fori(0, tiles // pairs) as i:
                        for q in range(pairs):
                            n, par = tiles0 + q, q % 2
                            for w in range(2):
                                dve.wait_ge(a_evac[l], 2 + 2 * n + w + 1 + 2 * pairs * i)
                                a, c = ca[:, par, w], cc[:, par, w, 0:CONV]
                                tap = [conv_w[:, l, w * FT + n + pairs * i, k:k + 1] for k in range(4)]
                                V.tensor_scalar(c, a[:, 1:1 + CONV], tap[1], tap[3], ALU.mult, ALU.add)
                                dve.drain()
                                V.scalar_tensor_tensor(out=c, in0=a[:, 0:CONV], scalar=tap[0], in1=c,
                                                       op0=ALU.mult, op1=ALU.add)
                                dve.drain()
                                V.scalar_tensor_tensor(out=c, in0=a[:, 2:2 + CONV], scalar=tap[2], in1=c,
                                                       op0=ALU.mult, op1=ALU.add).then_inc(conv_done[l], 1)
                            dve.drain()
                            dve.wait_ge(silu_done[l], n + 1 + pairs * i)
                            V.tensor_tensor(md[:, par, 0:NCTX], sg[:, par, 0:NCTX], cc[:, par, 0, 0:NCTX], ALU.mult)
                            V.tensor_tensor(md[:, par, NCTX:T], sg[:, par, LAT_AT:CONV], cc[:, par, 0, LAT_AT:CONV],
                                            ALU.mult).then_inc(md_done[l], 1)
                            dve.wait_ge(mhi_done[l], n + 1 + pairs * i)
                            V.tensor_tensor(m_l[:, pairs * i + q, :], md[:, par, :],
                                            m_h[:, pairs * i + q, :].bitcast(F32),
                                            ALU.subtract).then_inc(mlo_done[l], 1)
                            if b.ada and q == 0:
                                for blk in range(2):
                                    ada_copy(b, 4 * blk, i, blk, 12 + 8 * g + blk - 1 + 2 * i)
                            if b.ada and q == 1:
                                for blk in range(2):
                                    ada_mods(blk, 12 + 8 * g + blk + 1 + 2 * i, 1, 8 * g + blk + 2 * i)
                    tiles0 += tiles
                    residual(o0 + g, SEG["out", l, g], 0, 0, tiles, l, 5)
                dve.drain()

            dve.drain()
            norm_dve(1, 0, 3, 4)
            dve.wait_ge(st_stored, 32 * HEADS)
            ffn_phase(0, 4)
            norm_dve(2, 1, 0, 1)

            dve.wait_ge(at_in, 16 * AT_LOADS)
            V.tensor_copy(maskb[:], maskf[:])
            V.tensor_copy(identb[:], ident).then_inc(at_bf, 1)
            for j in range(10):
                dve.wait_ge(aqk_evac, j + 1)
                lat = lat_in[:, j % 4]
                V.stream_shuffle(swapped, lat, [(x + 16) % 32 for x in range(32)])
                V.tensor_tensor(r1, lat, rope_a[:, 0], ALU.mult)
                dve.drain()
                V.tensor_tensor(r2, swapped, rope_a[:, 1], ALU.mult)
                dve.drain()
                if j < 8:
                    op = V.tensor_tensor(aq[:, j, NCTX:T], r1, r2, ALU.add)
                else:
                    for r in range(2):
                        rows = slice(64 * r, 64 * r + 64)
                        op = V.tensor_tensor(ak[rows, 2 * (j - 8) + r, NCTX:T], r1[rows], r2[rows], ALU.add)
                op.then_inc(arope_done, 1)
                dve.drain()

            stat = small[:, 0:64].rearrange("p (a b) -> p a b", b=4)

            def unit_max(u):
                n, kv = divmod(u, KVH)
                w, st = P * len(key_blocks(n)), 8 * (u % 2)
                sink = vec[:, V_SINK + kv * G:V_SINK + (kv + 1) * G]
                dve.wait_ge(as_done, u + 1)
                V.tensor_reduce(stat[:, st, :], ps[:, 0:G, 0:w], AX.X, ALU.max)
                dve.drain()
                V.scalar_tensor_tensor(out=stat[:, st + 5, :], in0=stat[:, st, :], scalar=HD ** -0.5, in1=sink,
                                       op0=ALU.mult, op1=ALU.max)
                dve.drain()
                V.tensor_scalar(stat[:, st + 1, :], stat[:, st + 5, :], -1.0, None, ALU.mult)
                V.tensor_tensor(stat[:, st + 2, :], sink, stat[:, st + 5, :], ALU.subtract)
                dve.drain()
                V.tensor_copy(stat[:, st + 6, :], stat[:, st + 1, :]).then_inc(am_done, 1)

            def unit_norm(u):
                w, st = P * len(key_blocks(u // KVH)), 8 * (u % 2)
                dve.wait_ge(ae_done, u + 1)
                V.tensor_tensor(stat[:, st + 5, :], stat[:, st + 3, :], stat[:, st + 4, :], ALU.add)
                dve.drain()
                V.reciprocal(stat[:, st + 7, :], stat[:, st + 5, :])
                dve.drain()
                for g in range(G):
                    p = pr[:, u % 2, g, 0:w]
                    op = V.tensor_scalar(p, p, stat[:, st + 7, g:g + 1], None, ALU.mult)
                op.then_inc(ap_done, 1)

            unit_max(0)
            for u in range(UNITS):
                n = u // KVH
                unit_norm(u)
                if u + 1 < UNITS:
                    unit_max(u + 1)
                for kb in range(len(key_blocks(n))):
                    if (PT_AT[u] + kb) % 2 == 1:
                        dve.wait_ge(apt_done, PT_AT[u] + kb + 1)
                        if u >= 2:
                            dve.wait_ge(apv_done, u - 1)
                        V.tensor_copy(pT[:, u % 2, kb, :], ps[:, 5, :]).then_inc(apt_dve, 1)
                if u % 2 == 1:
                    o = u // 2
                    dve.wait_ge(aohi_done, o + 1)
                    at = slice((o % 2) * G, (o % 2) * G + G)
                    V.tensor_tensor(h_l[:, at, tok_of(n)], ps[:, 6 + o % 2, :].rearrange("p (g q) -> p g q", g=G),
                                    h_h[:, at, tok_of(n)].bitcast(F32), ALU.subtract).then_inc(aolo_done, 1)
            residual(7, SEG["att_o"], 0, 0, KT, 1, 2)
            dve.drain()
            norm_dve(3, 1, 3, 4)
            dve.wait_ge(kv_stored, 16 * 5)
            ffn_phase(1, 8)
            norm_dve(4, 1, 0, 0)


def _layout(x):
    import numpy as np
    f = np.float32
    a = {k: np.asarray(v) for k, v in x.items()}

    def feature(w):
        k, m = w.shape
        return w.reshape(k // P, P, m // P, P).transpose(2, 1, 0, 3).reshape(m // P, P, -1)

    def token(w):
        k, n = w.shape
        return w.reshape(k // 256, 2, P, n // 512, 512).transpose(3, 0, 2, 1, 4).reshape(-1, P, CH)

    dims = np.concatenate([np.arange(64), np.arange(128, 192), np.arange(64, 128), np.arange(192, 256)])
    ada0, ada1 = token(a["ada_w"][0]), token(a["ada_w"][1])
    parts = [ada0[0:16]]
    wo = token(a["ret_wo"][0])
    wo = wo.reshape(2, HEADS, 2, P, CH)
    for h in range(HEADS):
        q = feature(a["ret_wq"][0][:, h * DK + dims])
        k = feature(a["ret_wk"][0][:, h * DK + dims])
        parts += [q, k]
        if h:
            parts.append(wo[:, h - 1].reshape(4, P, CH))
        parts.append(ada0[16 + 8 * h:24 + 8 * h])
        for w in ("ret_wv", "ret_wg_fwd", "ret_wg_bwd"):
            parts.append(token(a[w][0][:, h * DV:(h + 1) * DV]))
    parts.append(wo[:, 3].reshape(4, P, CH))
    heads = [np.concatenate([np.arange(HD) + (kv * G + g) * HD for kv in (2 * p, 2 * p + 1)])
             for p in range(2) for g in range(G)]
    heads = np.concatenate(heads)
    for l in range(2):
        w_in = feature(a["ffn_w_in"][l])
        w_out = token(a["ffn_w_out"][l]).reshape(2, FT // 2, P, CH)
        t0 = 0
        ada = 0
        for g, tiles in enumerate(GROUPS):
            b = SEG["in", l, g]
            pairs = b.mains // 2
            for i in range(tiles // pairs):
                for q in range(pairs):
                    t = t0 + i * pairs + q
                    parts.append(w_in[[t, FT + t]])
                    if b.ada and q == 0:
                        parts.append(ada1[ada:ada + 8])
                        ada += 8
            parts.append(w_out[:, t0 // 2:(t0 + tiles) // 2].reshape(-1, P, CH))
            t0 += tiles
        if l == 0:
            parts.append(feature(a["attn_wq"][0][:, heads]))
            parts.append(feature(a["attn_wk"][0]))
            parts.append(a["attn_wv"][0].reshape(2, 4, P, KVH * HD).transpose(0, 2, 1, 3).reshape(2, P, CH))
            parts.append(token(a["attn_wo"][0][heads]))
    stream = np.concatenate(parts)
    assert stream.shape == (CHUNKS, P, CH), stream.shape

    vec = np.zeros((P, V_W), f)
    vec[:, V_C:V_C + 16] = np.stack([a["c"][0], a["c_ctx"]]).reshape(2, KT, P).transpose(2, 1, 0).reshape(P, 16)
    vec[:, V_ADAB:V_ADAB + 96] = a["ada_b"].reshape(2 * 48, P).T
    norms = [a["norm_mix"][0], a["norm_ffn"][0], a["norm_mix"][1], a["norm_ffn"][1], a["norm_final"]]
    vec[:, V_NORM:V_NORM + 40] = np.stack(norms).reshape(40, P).T
    vec[:, V_DEC:V_DEC + 4] = a["ret_decay_fwd"]
    vec[:, V_DEC + 4:V_DEC + 8] = a["ret_decay_bwd"]
    vec[:, V_SINK:V_SINK + QH] = a["attn_sink"]
    taps = np.concatenate([a["ffn_conv_w"], a["ffn_conv_b"][:, None]], axis=1)
    vec[:, V_CONV:] = taps.reshape(2, 4, 2 * FT, P).transpose(3, 0, 2, 1).reshape(P, -1)

    i = np.arange(P)
    cst = np.zeros((P, C_W), f)
    cst[:, C_ID:C_ID + P] = np.eye(P)
    cst[:, C_ONE:C_ONE + P] = 1
    for g in range(4):
        for s in range(2):
            cst[32 * g + s, C_SEL + s] = 1
    cst[:, C_ZF], cst[:, C_ZB] = P - 1 - i, i
    d = i[None, :] - i[:, None]
    diff = np.stack([np.maximum(d, 0), np.maximum(-d, 0)], 1).astype(f)
    tri = np.stack([d >= 0, d <= 0], 1).astype(f)
    iota = np.broadcast_to(np.stack([i + 1, P - i]), (P, 2, P)).astype(f)
    mask = np.stack([np.where(d >= 0, 0, NEG), np.where(d <= 0, 0, NEG)], 1).astype(f)
    t = np.arange(NLAT)
    rows, cols = (t // 64).astype(f), (t % 64).astype(f)

    def table(freq, is_row, n, sign):
        inv = (f(10000.0) ** (-np.arange(n, dtype=f) / f(n))).astype(f)
        pos = np.where(is_row[:, None], rows[None], cols[None]).astype(f)
        ang = (pos * inv[freq][:, None]).astype(f)
        return np.stack([np.cos(ang), np.sin(ang) * sign[:, None]], 1).astype(f)

    rope_t = table(i % 64, i < 64, 64, np.ones(P, f))
    rope_a = table(i % 16, i % 64 < 32, 16, np.where(i % 32 < 16, -1, 1).astype(f))
    xs = np.concatenate([a["x_prompt"][0], a["x_sample"][0]])
    st = np.stack([a["state_ret_fwd"][0, 0], a["state_ret_bwd"][0, 0]])[:, :, dims]
    return {
        "stream": stream, "vec": vec, "cst": cst,
        "x": xs.reshape(T, KT, P).transpose(2, 1, 0),
        "diff": np.broadcast_to(diff[:, :, None], (P, 2, HEADS, P)), "tri": tri, "iota": iota,
        "rope_t": rope_t, "rope_a": rope_a, "mask": mask,
        "state": st.reshape(2, HEADS, 2, P, DV).transpose(1, 3, 0, 2, 4),
        "cache_v": a["cache_attn_v"][0, 0].reshape(NCTX, KVH * HD),
        "cache_k": a["cache_attn_k"][0, 0].transpose(1, 2, 0),
    }, dims


_OUTS = {"y": (KT, P, T), "new_state": (2, HEADS, P, 2, DV), "new_k": (KVH, HD, NCTX), "new_v": (NCTX, KVH * HD)}


def kernel(**inputs):
    import numpy as np
    import concourse.bacc as bacc
    from concourse.bass_utils import run_bass_kernel_spmd as run

    arrays, dims = _layout(inputs)
    arrays = {k: np.ascontiguousarray(x) for k, x in arrays.items()}
    nc = bacc.Bacc("TRN2", target_bir_lowering=False, num_devices=1)
    dr = {k: nc.dram_tensor(k + "_dram", x.shape, F32, kind="ExternalInput").ap() for k, x in arrays.items()}
    for k, shape in _OUTS.items():
        dr[k] = nc.dram_tensor(k + "_dram", shape, F32, kind="ExternalOutput").ap()
    build(nc, dr)
    got = run(nc, [{k + "_dram": x for k, x in arrays.items()}], core_ids=[0]).results[0]
    y = got["y_dram"].reshape(D, T).T
    state = np.empty((2, HEADS, DK, DV), np.float32)
    state[:, :, dims] = got["new_state_dram"].transpose(0, 1, 3, 2, 4).reshape(2, HEADS, DK, DV)
    k = got["new_k_dram"].transpose(2, 0, 1)
    return (np.ascontiguousarray(y[:NCTX])[None], np.ascontiguousarray(y[NCTX:])[None],
            state[0][None, None], state[1][None, None],
            np.ascontiguousarray(k)[None, None], got["new_v_dram"].reshape(1, 1, NCTX, KVH, HD))
```

```python
from contextlib import ExitStack

import concourse.bass as bass
from concourse import mybir

F32 = mybir.dt.float32
F32R = mybir.dt.float32r
BF16 = mybir.dt.bfloat16
ALU = mybir.AluOpType
ACT = mybir.ActivationFunctionType
AX = mybir.AxisListType

P = 128
D = 1024
KT = D // P
NCTX, NLAT = 128, 512
T = NCTX + NLAT
TT = T // P
HALF = T // 2
CUT = HALF - NCTX
HEADS, DK, DV = 4, 256, 512
QH, KVH, HD = 16, 4, 64
G = QH // KVH
FF = 2816
FT = FF // P
GROUPS = (8, 8, 6)
EPS = 1e-6
NEG = -1e30
RAW = 4
RING = 2
CH = 8 * P
PAD = T + 3
CONV = T + 1
LAT_AT = NCTX + 1

C_ID, C_ONE, C_SEL, C_ZF, C_ZB = 0, 128, 256, 258, 259
C_W = 260
V_C, V_ADAB, V_NORM, V_DEC, V_SINK = 0, 16, 112, 152, 160
V_CONV = 176
V_W = V_CONV + 2 * 2 * FT * 4


class Body:

    def __init__(self, c0, m0, kinds):
        self.c0, self.m0, self.kinds = c0, m0, kinds
        self.raw, self.mains = len(kinds), kinds.count("m")
        self.at = [k for k, x in enumerate(kinds) if x == "m"] + [len(kinds), len(kinds) + 1]
        self.ada = [k for k, x in enumerate(kinds) if x == "a"]

    def chunk(self, k, i):
        c = self.c0 + k
        return c % RAW, c // RAW + 1 + (self.raw // RAW) * i

    def split(self, j, i):
        m = self.m0 + j
        return m % RING, m // RING + 1 + (self.mains // RING) * i

    def done(self, j, i):
        return self.m0 + j + 1 + self.mains * i


def plan():
    seg = {}
    seg["ret0"] = Body(16, 0, "mmaaaammmaaaa" + "m" * 11)
    seg["ret"] = Body(40 - 28, 16 - 20, "mmaaaammmmmmmaaaa" + "m" * 11)
    seg["wo3"] = Body(124, 76, "mmmm")
    c, m = 128, 80
    for layer in range(2):
        for g, tiles in enumerate(GROUPS):
            kinds = "mmmm"
            if layer == 0 and g == 0:
                kinds = "mmaaaammaaaa"
            if layer == 0 and g == 1:
                kinds = "mmmmaaaa"
            b = Body(c, m, kinds)
            seg["in", layer, g] = b
            turns = 2 * tiles // b.mains
            c, m = c + turns * b.raw, m + turns * b.mains
            seg["out", layer, g] = Body(c, m, "m" * tiles)
            c, m = c + tiles, m + tiles
        if layer == 0:
            seg["att"] = Body(c, m, "m" * 12)
            seg["att_o"] = Body(c + 12, m + 12, "m" * 8)
            c, m = c + 20, m + 20
    return seg, c, m


SEG, CHUNKS, MAINS = plan()
Y_ORDER = (0, 3, 2, 4, 1)
AT_LOADS = 3 + KVH
UNITS = (TT) * KVH


def band(n):
    return max(n - 1, 0), min(n + 2, NLAT // P)


def key_blocks(n):
    return [0] if n == 4 else [None] + [1 + b for b in range(*band(n))]


def tok_of(n):
    return slice(0, NCTX) if n == 4 else slice(NCTX + n * P, NCTX + (n + 1) * P)


POOL_LO = (1, 3, 5, 6)
PT_ACT = (1, 2)
PT_AT = [sum(len(key_blocks(x // KVH)) for x in range(u)) for u in range(UNITS)]

PT_OF = [kb in PT_ACT for u in range(UNITS) for kb in range(len(key_blocks(u // KVH)))]


def over(ap, n):
    return ap.unsqueeze(1).to_broadcast([ap.shape[0], n, ap.shape[1]])


def build(nc, dr):
    with ExitStack() as ctx:
        def sb(name, shape, dt=F32, where=ctx):
            return where.enter_context(nc.sbuf_tensor(name, shape, dt))

        def sem(name):
            return ctx.enter_context(nc.semaphore(name))

        ps = ctx.enter_context(nc.psum_tensor("ps", [P, 8, 512], F32))

        xT = sb("xT", [P, KT, T])
        raw = sb("raw", [P, RAW, CH])
        w_h, w_l = sb("w_h", [P, RING, CH], F32R), sb("w_l", [P, RING, CH], F32R)
        h_h, h_l = sb("h_h", [P, KT, T], F32R), sb("h_l", [P, KT, T], F32R)
        cst = sb("cst", [P, C_W])
        vec = sb("vec", [P, V_W])
        mods = sb("mods", [P, 2, 48, 2])
        mod_a = sb("mod_a", [P, KT, 2])
        csil = sb("csil", [P, KT, 32])
        ada_o = sb("ada_o", [P, 2, 512])
        small = sb("small", [P, 104])
        front = sb("front", [P, 8 * T])
        ident, ones, sel = cst[:, C_ID:C_ID + P], cst[:, C_ONE:C_ONE + P], cst[:, C_SEL:C_SEL + 2]
        eps = small[:, 95:96]
        conv_w = vec[:, V_CONV:V_W].rearrange("p (l t k) -> p l t k", l=2, k=4)
        ada_b = vec[:, V_ADAB:V_ADAB + 96].rearrange("p (l t) -> p l t", l=2)
        norm_g = vec[:, V_NORM:V_NORM + 40].rearrange("p (n t) -> p n t", n=5)
        sq_sum = front[:, 0:T]
        diag = front[:, T:2 * T].rearrange("p (t q) -> p t q", t=TT)
        xn = front[:, 2 * T:4 * T].rearrange("p (b t) -> p b t", b=2)
        hf = front[:, 4 * T:8 * T].rearrange("p (b t) -> p b t", b=4)
        sq = hf[:, 0:2]
        root, r_rms = small[:, 86:86 + TT], small[:, 96:96 + TT]
        ms_ps = ps[:, 7, 256:256 + TT]
        rstd = ps[:, 6:8, :].rearrange("p b t -> p (b t)")[:, 0:T]

        with ExitStack() as ret:
            v = front[:, 0:TT * 512].rearrange("p (t d) -> p t d", t=TT)
            gf = front[:, TT * 512:2 * TT * 512].rearrange("p (t d) -> p t d", t=TT)
            gb = sb("gb", [P, TT, 512], F32, ret)
            qT, kT = sb("qT", [P, 2, T], F32, ret), sb("kT", [P, 2, T], F32, ret)
            qf = sb("qf", [P, 2, NLAT], F32, ret)
            S = sb("S", [P, 2, 2, DV], F32, ret)
            kz = sb("kz", [P, 2, 4, DK], F32, ret)
            rope_t = sb("rope_t", [P, 2, NLAT], F32, ret)
            dm = sb("dm", [P, 2, HEADS, P], F32, ret)
            xi = sb("xi", [P, 2, HEADS, P], F32, ret)
            st_out = sb("st_out", [P, 2, 2, DV], F32, ret)
            junk = sb("junk", [P, 512], F32, ret)
            y_h, y_l = sb("y_h", [P, 4, T], F32R, ret), sb("y_l", [P, 4, T], F32R, ret)
        with ExitStack() as ffn:
            ca = sb("ca", [P, 2, 2, PAD + 1], F32, ffn)
            cc = sb("cc", [P, 2, 2, CONV + 1], F32, ffn)
            sg = sb("sg", [P, 2, CONV + 1], F32, ffn)
            md = sb("md", [P, 2, T], F32, ffn)
            m_h, m_l = sb("m_h", [P, 8, T], F32R, ffn), sb("m_l", [P, 8, T], F32R, ffn)
        with ExitStack() as att:
            aq = sb("aq", [P, KT, T], F32, att)
            ak = sb("ak", [P, KVH, T], F32, att)
            ck = sb("ck", [P, KVH, NCTX], F32, att)
            av = sb("av", [P, TT, KVH * HD], F32, att)
            cv = sb("cv", [P, KVH * HD], F32, att)
            rope_a = sb("rope_a", [P, 2, NLAT], F32, att)
            maskf = sb("maskf", [P, 2, P], F32, att)
            maskb = sb("maskb", [P, 2, P], BF16, att)
            identb = sb("identb", [P, P], BF16, att)
            pr = sb("pr", [P, 2, G, 512], F32, att)
            pT = sb("pT", [P, 2, 4, 512], F32, att)
        lat_in = front[:, 0:4 * NLAT].rearrange("p (b t) -> p b t", b=4)
        swapped = front[:, 4 * NLAT:5 * NLAT]
        r1, r2 = front[:, 5 * NLAT:6 * NLAT], front[:, 6 * NLAT:7 * NLAT]

        iota = st_out[:, 0, 0, 0:2 * P].rearrange("p (d i) -> p d i", d=2)
        tri = st_out[:, 0, 1, 0:2 * P].rearrange("p (d i) -> p d i", d=2)

        raw_landed = [sem(f"raw_landed{s}") for s in range(RAW)]
        raw_used = [sem(f"raw_used{s}") for s in range(RAW)]
        hi_ready = [sem(f"hi_ready{s}") for s in range(RING)]
        chunk_done = sem("chunk_done")
        const_in, vec_in, x_in = sem("const_in"), sem("vec_in"), sem("x_in")
        eps_set = sem("eps_set")
        csil_zero, csil_ready = sem("csil_zero"), sem("csil_ready")
        ada_copied, ada_turned, mods_done = sem("ada_copied"), sem("ada_turned"), sem("mods_done")
        a_ready = sem("a_ready")
        sq_done, sq_added, sum_done, root_done = (sem(n) for n in ("sq_done", "sq_added", "sum_done", "root_done"))
        diag_done, rstd_done = sem("diag_done"), sem("rstd_done")
        hf_done, hhi_done = sem("hf_done"), sem("hhi_done")
        hlo_pool, hlo_dve = sem("hlo_pool"), sem("hlo_dve")
        out_done = sem("out_done")
        res_done = sem("res_done")
        dec_in, dec_abs, dec_e, dec_w, dec_ln, dec_lg = (sem(f"dec_{n}") for n in
                                                         ("in", "abs", "e", "w", "ln", "lg"))
        dec_exp, dec_ready = sem("dec_exp"), sem("dec_ready")
        rope_in = sem("rope_in")
        qk_evac, rope_done, tile_done, tok_evac = (sem(n) for n in ("qk_evac", "rope_done", "tile_done", "tok_evac"))
        scores_read = sem("scores_read")
        scores_done, sT_done, kz_done, S_in = (sem(n) for n in ("scores_done", "sT_done", "kz_done", "S_in"))
        o_done, u_done, S_upd, st_copied, st_stored = (sem(n) for n in
                                                       ("o_done", "u_done", "S_upd", "st_copied", "st_stored"))
        ss_done, rms_done, o_evac, y_done = (sem(n) for n in ("ss_done", "rms_done", "o_evac", "y_done"))
        yT_done, yhi_done, ylo_done = sem("yT_done"), sem("yhi_done"), sem("ylo_done")
        a_evac = [sem(f"a_evac{l}") for l in range(2)]
        conv_done = [sem(f"conv_done{l}") for l in range(2)]
        silu_done = [sem(f"silu_done{l}") for l in range(2)]
        md_done = [sem(f"md_done{l}") for l in range(2)]
        mhi_done = [sem(f"mhi_done{l}") for l in range(2)]
        mlo_done = [sem(f"mlo_done{l}") for l in range(2)]
        at_zero, at_in, at_bf, aqk_evac, arope_done = (sem(n) for n in
                                                       ("at_zero", "at_in", "at_bf", "aqk_evac", "arope_done"))
        atile_done, av_evac, as_done, am_done, ae_done, ap_done = (
            sem(n) for n in ("atile_done", "av_evac", "as_done", "am_done", "ae_done", "ap_done"))
        apt_done, apt_act, apt_dve, apv_done, aohi_done, aolo_done = (
            sem(n) for n in ("apt_done", "apt_act", "apt_dve", "apv_done", "aohi_done", "aolo_done"))
        y_scaled, y_stored, kv_stored = sem("y_scaled"), sem("y_stored"), sem("kv_stored")

        block = ctx.enter_context(nc.Block())

        def lo_hi(b):
            return slice(b * HALF, b * HALF + HALF)

        def wait_pt(eng, x):
            eng.wait_ge(apt_act if PT_OF[x] else apt_dve, sum(y == PT_OF[x] for y in PT_OF[:x + 1]))

        def wait_rest(eng, n, k):
            if k in POOL_LO:
                eng.wait_ge(hlo_pool, len(POOL_LO) * n + POOL_LO.index(k) + 1)
            else:
                eng.wait_ge(hlo_dve, (KT - len(POOL_LO)) * n + k + 1 - sum(p < k for p in POOL_LO))

        def ada_at(b, g, q, i):
            if not b.ada or (g == 1 and q == 0):
                return None
            return 12 + q + 2 * i if g == 0 else 20 + i

        def out_bank(mh, at):
            return (at + 4) % 8 if mh == 0 else at

        def spans(b):
            if b == 0:
                return [(slice(0, NCTX), slice(0, NCTX), 1), (slice(NCTX, HALF), slice(NCTX, HALF), 0)]
            return [(slice(0, HALF), slice(HALF, T), 0)]

        @block.sync
        def _(sp):
            def load(c, i, turns):
                s = c % RAW
                if turns is not None:
                    sp.wait_ge(raw_used[s], turns)
                sp.dma_start(raw[:, s, :], dr["stream"][c + RAW * i]).then_inc(raw_landed[s], 16)

            for c in range(RAW):
                load(c, 0, None)
            with sp.Fori(1, CHUNKS // RAW) as i:
                for c in range(RAW):
                    load(c, i, i)
            sp.wait_ge(y_stored, 16 * KT)
            sp.wait_ge(st_stored, 32 * HEADS)
            sp.wait_ge(kv_stored, 16 * 5)

        @block.tensor
        def _(pe):
            def weights(b, j, i):
                s, n = b.split(j, i)
                pe.wait_ge(hi_ready[s], n)
                c, used = b.chunk(b.at[j], i)
                pe.wait_ge(raw_used[c], used)
                return s

            def feature_tile(b, j, i, banks, free, norm=None):
                s = weights(b, j, i)
                if norm is not None:
                    free(0)
                    free(1)
                    for k in range(KT):
                        wait_rest(pe, norm, k)
                        wh, wl = (w[:, s, k * P:(k + 1) * P] for w in (w_h, w_l))
                        for half in range(2):
                            for n, (w, x) in enumerate(((wh, h_h), (wh, h_l), (wl, h_h))):
                                mm = nc.tensor.matmul(ps[:, banks + half, 0:HALF], w, x[:, k, lo_hi(half)],
                                                      start=(k == 0 and n == 0), stop=(k == KT - 1 and n == 2))
                    mm.then_inc(chunk_done, 1)
                    return
                for half in range(2):
                    free(half)
                    for k in range(KT):
                        wh, wl = (w[:, s, k * P:(k + 1) * P] for w in (w_h, w_l))
                        for n, (w, x) in enumerate(((wh, h_h), (wh, h_l), (wl, h_h))):
                            mm = nc.tensor.matmul(ps[:, banks + half, 0:HALF], w, x[:, k, lo_hi(half)],
                                                  start=(k == 0 and n == 0), stop=(k == KT - 1 and n == 2))
                mm.then_inc(chunk_done, 1)

            def token_chunk(b, j, i, kc, ks, n_cols, bank, free):
                s = weights(b, j, i)
                last = kc == KT // ks - 1
                for t in range(TT):
                    if kc == 0:
                        free(t)
                    for kk in range(ks):
                        k = kc * ks + kk
                        wh, wl = (w[:, s, kk * n_cols:(kk + 1) * n_cols] for w in (w_h, w_l))
                        for n, (x, w) in enumerate(((h_h, wh), (h_h, wl), (h_l, wh))):
                            mm = nc.tensor.matmul(ps[:, bank(t), 0:n_cols], x[:, k, t * P:(t + 1) * P], w,
                                                  start=(k == 0 and n == 0), stop=(k == KT - 1 and n == 2))
                    if t == TT - 1:
                        mm.then_inc(chunk_done, 1)
                    elif last:
                        mm.then_inc(tile_done if n_cols == 512 else atile_done, 1)

            def out_proj(b, j0, i, tiles, xh, xl, ready, free):
                j = j0
                for mh in range(2):
                    for kc in range(tiles // 2):
                        s = weights(b, j, i)
                        ready(kc)
                        for at in range(8):
                            bank = out_bank(mh, at)
                            mt, half = bank // 2, bank % 2
                            if kc == 0:
                                free(mh, bank)
                            for kk in range(2):
                                k = 2 * kc + kk
                                c = kk * 512 + mt * P
                                wh, wl = w_h[:, s, c:c + P], w_l[:, s, c:c + P]
                                for n, (w, x) in enumerate(((wh, xh), (wh, xl), (wl, xh))):
                                    mm = nc.tensor.matmul(ps[:, bank, 0:HALF], w, x[:, k, lo_hi(half)],
                                                          start=(k == 0 and n == 0),
                                                          stop=(k == tiles - 1 and n == 2))
                            if kc == tiles // 2 - 1 and at < 7:
                                mm.then_inc(out_done, 1)
                        mm.then_inc(chunk_done, 1)
                        j += 1

            def ada_block(b, k0, i, par):
                for kc in range(4):
                    s, n = b.chunk(b.ada[k0 + kc], i)
                    pe.wait_ge(raw_landed[s], 16 * n)
                    for kk in range(2):
                        k = 2 * kc + kk
                        g = k % 4
                        mm = nc.tensor.matmul(ps[32 * g:32 * g + 32, 4 + par, :], csil[:, k, :],
                                              raw[:, s, kk * 512:(kk + 1) * 512], start=(k < 4), stop=(k >= 4))
                    mm.then_inc(raw_used[s], 1)

            def ada_turn(par, copied):
                pe.wait_ge(ada_copied, copied)
                for f in range(4):
                    mm = nc.tensor.matmul(ps[:, 4 + par, 2 * f:2 * f + 2],
                                          ada_o[:, par, f * P:(f + 1) * P], sel, start=True, stop=True)
                mm.then_inc(ada_turned, 1)

            def norm_sum(n, free):
                free()
                pe.wait_ge(sq_added, (KT - 3) * (n + 1))
                pe.wait_ge(sq_done, KT * (n + 1))
                for t in range(TT):
                    for k in range(KT - 3, KT):
                        src = sq_sum if k == KT - 3 else sq[:, k % 2]
                        mm = nc.tensor.matmul(ms_ps[:, t:t + 1], src[:, t * P:(t + 1) * P], ones[:, 0:1],
                                              start=(k == KT - 3), stop=(k == KT - 1))
                mm.then_inc(sum_done, 1)
                for t in range(TT):
                    pe.wait_ge(diag_done, TT * n + t + 1)
                    nc.tensor.matmul(rstd[:, t * P:(t + 1) * P], ones, diag[:, t], start=True,
                                     stop=True).then_inc(rstd_done, 1)

            pe.wait_ge(const_in, 16)
            pe.wait_ge(csil_ready, 1)
            first = Body(0, 0, "a" * 16)
            for blk in range(4):
                if blk >= 2:
                    pe.wait_ge(mods_done, blk - 1)
                ada_block(first, 4 * blk, 0, blk % 2)
                ada_turn(blk % 2, blk + 1)
                if blk == 2:
                    norm_sum(0, lambda: None)

            def head(b, h, first_head):
                for j in range(4):
                    def free(half, j=j):
                        if half:
                            return
                        if j >= 2:
                            pe.wait_ge(qk_evac, 4 * h + j - 1)
                        elif not first_head:
                            pe.wait_ge(S_upd, 6 * h)
                    feature_tile(b, j, h, 2 * (j % 2), free, 0 if first_head and j == 0 else None)
                    if j == 0:
                        pe.wait_ge(mods_done, 4 + 2 * h)
                        ada_block(b, 0, h, 0)
                    if j == 1:
                        ada_turn(0, 4 + 2 * h + 1)
                    if not first_head and j in (1, 2):
                        turn_y(h - 1, (0, 1, 2) if j == 1 else (3, 4))
                j = 4
                if not first_head:
                    pe.wait_ge(ylo_done, TT * (h - 1) + TT)
                    pe.wait_ge(mods_done, 4 + 2 * h + 1)
                    out_proj(b, 4, h, 4, y_h, y_l, lambda kc: None, free_out(h - 1, h))
                    j = 8
                if not first_head:
                    pe.wait_ge(res_done, 16 * (h - 1) + 14)
                pe.wait_ge(mods_done, 4 + 2 * h + 1)
                ada_block(b, 4, h, 1)
                pe.wait_ge(qk_evac, 4 * h + 4)
                for proj in range(3):
                    for kc in range(4):
                        def free(t, proj=proj):
                            if proj > 0:
                                pe.wait_ge(tok_evac, 15 * h + 5 * (proj - 1) + t + 1)
                                if t == 3 and proj == 1:
                                    pe.wait_ge(scores_read, h + 1)
                                if t == 4 and proj == 1:
                                    pe.wait_ge(kz_done, h + 1)
                        token_chunk(b, j, h, kc, 2, 512, lambda t: t, free)
                        j += 1
                        if proj == 0 and kc == 0:
                            ada_turn(1, 4 + 2 * h + 2)
                    if proj == 0:
                        scores(h)
                steps(h)

            def scores(h):
                pe.wait_ge(rope_done, 2 * h + 2)
                pe.wait_ge(mods_done, 4 + 2 * h + 2)
                pe.wait_ge(tok_evac, 15 * h + 5)
                for c in range(TT):
                    for t in range(2):
                        tok = slice(c * P, (c + 1) * P)
                        out = ps[:, 3, 0:P] if c == 0 else ps[:, 5, (c - 1) * P:c * P]
                        nc.tensor.matmul(out, kT[:, t, tok], qT[:, t, tok], start=(t == 0), stop=(t == 1))
                for c in range(TT):
                    for t in range(2):
                        bank, col = ((6, P), (7, 0), (7, DK), (4, 0), (4, DK))[c]
                        mm = nc.tensor.transpose(ps[:, bank, col + t * P:col + (t + 1) * P],
                                                 kT[:, t, c * P:(c + 1) * P], ident)
                mm.then_inc(scores_done, 1)

            def steps(h):
                pe.wait_ge(sT_done, h + 1)
                pe.wait_ge(tok_evac, 15 * h + 15)
                pe.wait_ge(S_in, 16 * h + 16)
                for d in range(2):
                    nc.tensor.matmul(ps[:, 6 + d, :], kT[:, d, 0:P], v[:, 0, :],
                                     start=True, stop=True).then_inc(o_done, 1)
                for d in range(2):
                    for t in range(2):
                        mm = nc.tensor.matmul(ps[:, 2 * d + t, :], kz[:, d, 0, t * P:(t + 1) * P], v[:, 0, :],
                                              start=True, stop=True)
                    mm.then_inc(u_done, 1)
                for s in range(4):
                    for d in range(2):
                        c = s if d == 0 else 3 - s
                        q = qf if d == 0 else qT[:, :, NCTX:T]
                        pe.wait_ge(o_evac, 10 * h + 2 * s + d + 1)
                        nc.tensor.matmul(ps[:, 6 + d, :], kT[:, d, (c + 1) * P:(c + 2) * P], v[:, c + 1, :],
                                         start=True, stop=False)
                        if s >= 1:
                            pe.wait_ge(S_upd, 6 * h + 2 * (s - 1) + d + 1)
                        for t in range(2):
                            mm = nc.tensor.matmul(ps[:, 6 + d, :], q[:, t, c * P:(c + 1) * P], S[:, d, t, :],
                                                  start=False, stop=(t == 1))
                        mm.then_inc(o_done, 1)
                        if s == 3:
                            continue
                        if s == 0:
                            pe.wait_ge(st_copied, 2 * h + d + 1)
                        slot = c + 1 if d == 0 else c
                        for t in range(2):
                            mm = nc.tensor.matmul(ps[:, 2 * d + t, :], kz[:, d, slot, t * P:(t + 1) * P],
                                                  v[:, c + 1, :], start=True, stop=True)
                        mm.then_inc(u_done, 1)

            def turn_y(h, ns):
                for n in ns:
                    t = Y_ORDER[n]
                    pe.wait_ge(y_done, TT * h + n + 1)
                    if n >= 3:
                        pe.wait_ge(ylo_done, TT * h + n - 2)
                    elif n >= 1:
                        pe.wait_ge(o_evac, 10 * h + 8 + n)
                    for k in range(4):
                        mm = nc.tensor.transpose(ps[:, 5 + n % 3, k * P:(k + 1) * P],
                                                 gf[:, t, k * P:(k + 1) * P], ident)
                    mm.then_inc(yT_done, 1)

            def free_out(o, h):
                def free(mh, bank):
                    if mh == 1:
                        pe.wait_ge(res_done, 16 * o + (bank + 4) % 8 + 1)
                    elif bank == 0 and h is not None:
                        pe.wait_ge(qk_evac, 4 * h + 4)
                return free

            head(SEG["ret0"], 0, True)
            with pe.Fori(1, HEADS) as h:
                head(SEG["ret"], h, False)
            turn_y(HEADS - 1, range(TT))
            pe.wait_ge(ylo_done, TT * HEADS)
            out_proj(SEG["wo3"], 0, 0, 4, y_h, y_l, lambda kc: None, free_out(3, None))

            def ffn_phase(l, o0):
                tiles0 = 0
                for g, tiles in enumerate(GROUPS):
                    b = SEG["in", l, g]
                    pairs = b.mains // 2

                    def pair_group(i, l=l, g=g, b=b, pairs=pairs, tiles0=tiles0):
                        for q in range(pairs):
                            n = tiles0 + q
                            for w in range(2):
                                def free(half, w=w, n=n):
                                    if half == 0:
                                        pe.wait_ge(a_evac[l], 2 * n + w + 1 + 2 * pairs * i)
                                first = g == 0 and q == 0 and w == 0
                                feature_tile(b, 2 * q + w, i, 2 * w, free, 1 + 2 * l if first else None)
                                blk = ada_at(b, g, q, i)
                                if blk is not None and w == 0:
                                    pe.wait_ge(mods_done, blk)
                                    ada_block(b, 4 * q if g == 0 else 0, i, q)
                                if blk is not None and w == 1:
                                    ada_turn(q, blk + 1)

                    with pe.Fori(0, tiles // pairs) as i:
                        pair_group(i)
                    if b.ada:
                        pe.wait_ge(mods_done, (20, 24)[g])
                    done = tiles0 + tiles

                    def ready(kc, l=l, done=done, tiles=tiles):
                        pe.wait_ge(mlo_done[l], done - tiles + 2 * kc + 2)

                    def free(mh, bank, l=l, done=done, o=o0 + g):
                        if mh == 1:
                            pe.wait_ge(res_done, 16 * o + (bank + 4) % 8 + 1)
                        elif bank == 4:
                            pe.wait_ge(res_done, 16 * o)
                        elif bank == 0:
                            pe.wait_ge(a_evac[l], 2 + 2 * done)
                    out_proj(SEG["out", l, g], 0, 0, tiles, m_h, m_l, ready, free)
                    tiles0 = done
                    if g < 2:
                        pe.wait_ge(res_done, 16 * (o0 + g) + (14 if SEG["in", l, g + 1].ada else 12))

            def free_norm(o):
                return lambda: pe.wait_ge(res_done, 16 * (o + 1))

            norm_sum(1, free_norm(3))
            ffn_phase(0, 4)
            norm_sum(2, free_norm(6))

            b = SEG["att"]
            for j in range(10):
                def free(half, j=j):
                    if half == 0 and j >= 2:
                        pe.wait_ge(aqk_evac, j - 1)
                feature_tile(b, j, 0, 2 * (j % 2), free, 2 if j == 0 else None)
            for kc in range(2):
                def free(t):
                    if t == 4:
                        pe.wait_ge(aqk_evac, 9)
                token_chunk(b, 10 + kc, 0, kc, 4, KVH * HD, lambda t: (4 + t) % 8, free)
            pe.wait_ge(aqk_evac, 10)
            pe.wait_ge(av_evac, TT)
            pe.wait_ge(arope_done, 10)
            pe.wait_ge(at_in, 16 * AT_LOADS)
            pe.wait_ge(at_bf, 1)

            def unit_scores(u):
                n, kv = divmod(u, KVH)
                for g in range(G):
                    if u >= 1 and g % 2 == 0:
                        pe.wait_ge(ae_done, 2 * (u - 1) + g // 2 + 1)
                    q = aq[:, (kv // 2) * G + g, tok_of(n)]
                    if n == 4:
                        mm = nc.tensor.matmul(ps[:, g, 0:P], q, ak[:, kv, 0:NCTX], start=True, stop=True)
                    else:
                        nc.tensor.matmul(ps[:, g, 0:P], q, ck[:, kv, :], start=True, stop=True)
                        lo, hi = band(n)
                        nc.tensor.matmul(ps[:, g, P:P * (1 + hi - lo)], q, ak[:, kv, NCTX + lo * P:NCTX + hi * P],
                                         start=True, stop=False)
                        if n > lo:
                            mm = nc.tensor.matmul(ps[:, g, P:2 * P], identb[:], maskb[:, 0, :], start=False,
                                                  stop=(n + 1 >= hi))
                        if n + 1 < hi:
                            mm = nc.tensor.matmul(ps[:, g, P * (hi - lo):P * (hi - lo + 1)], identb[:],
                                                  maskb[:, 1, :], start=False, stop=True)
                    if g % 2 == 1:
                        mm.then_inc(as_done, 1)

            def unit_turn(u, kb):
                x = PT_AT[u] + kb
                if x >= 3:
                    wait_pt(pe, x - 3)
                for g in range(G):
                    mm = nc.tensor.transpose(ps[:, 4 + x % 3, g * P:(g + 1) * P],
                                             pr[:, u % 2, g, kb * P:(kb + 1) * P], ident)
                mm.then_inc(apt_done, 1)

            def unit_values(u):
                n, kv = divmod(u, KVH)
                kbs = key_blocks(n)
                pe.wait_ge(ap_done, u + 1)
                for kb in range(min(3, len(kbs))):
                    unit_turn(u, kb)
                if kv % 2 == 0 and u >= 2:
                    pe.wait_ge(aolo_done, u // 2)
                for kb, src in enumerate(kbs):
                    if kb == 1 and len(kbs) > 3:
                        unit_turn(u, 3)
                    wait_pt(pe, PT_AT[u] + kb)
                    val = cv if src is None else av[:, src, :]
                    mm = nc.tensor.matmul(ps[64 * (kv % 2):64 * (kv % 2) + 64, 7, :],
                                          val[:, kv * HD:(kv + 1) * HD], pT[:, u % 2, kb, :],
                                          start=(kb == 0), stop=(kb == len(kbs) - 1))
                mm.then_inc(apv_done, 1)

            unit_scores(0)
            for u in range(UNITS):
                if u + 1 < UNITS:
                    unit_scores(u + 1)
                unit_values(u)
            pe.wait_ge(aolo_done, UNITS // 2)
            pe.wait_ge(ae_done, 2 * UNITS)

            def free(mh, bank):
                if mh == 1:
                    pe.wait_ge(res_done, 16 * 7 + (bank + 4) % 8 + 1)
            out_proj(SEG["att_o"], 0, 0, KT, h_h, h_l, lambda kc: None, free)
            norm_sum(3, free_norm(7))
            ffn_phase(1, 8)
            norm_sum(4, free_norm(10))

        @block.scalar
        def _(act):
            def hi(b, j, i):
                if b is None:
                    return
                s, landed = b.chunk(b.at[j], i)
                r, n = b.split(j, i)
                act.wait_ge(raw_landed[s], 16 * landed)
                if not (b.m0 + j < RING and isinstance(i, int)):
                    act.wait_ge(chunk_done, b.done(j, i) - RING)
                nc.scalar.copy(w_h[:, r, :], raw[:, s, :]).then_inc(hi_ready[r], 1)

            act.dma_start(vec[:], dr["vec"]).then_inc(vec_in, 16)
            act.dma_start(xT[:], dr["x"]).then_inc(x_in, 16)
            act.dma_start(cst[:], dr["cst"]).then_inc(const_in, 16)
            act.wait_ge(vec_in, 16)
            act.wait_ge(csil_zero, 1)
            cvec = vec[:, V_C:V_C + 16].rearrange("p (k s) -> p k s", s=2)
            nc.scalar.activation(csil[:, :, 0:2], cvec, ACT.Silu).then_inc(csil_ready, 1)

            def norm_squares(n, ks, ready):
                for k in ks:
                    ready(k)
                    if k == 0:
                        nc.scalar.activation(small[:, 82:83], eps, ACT.Sqrt)
                    if k >= 2:
                        act.wait_ge(sq_added, (KT - 3) * n + max(k - 2, 1))
                    nc.scalar.activation(sq[:, k % 2, :], xT[:, k, :], ACT.Square).then_inc(sq_done, 1)

            def norm_root(n):
                act.wait_ge(sum_done, n + 1)
                nc.scalar.activation(root, ms_ps, ACT.Sqrt, bias=eps, scale=1.0 / D).then_inc(root_done, 1)

            def norm_hi(n):
                for k in range(KT):
                    act.wait_ge(hf_done, KT * n + k + 1)
                    nc.scalar.copy(h_h[:, k, :], hf[:, k % 4, :]).then_inc(hhi_done, 1)

            def out_act(b, tiles, n, ready):
                for j in range(tiles):
                    if n is not None and j == tiles - 2:
                        norm_squares(n, range(KT // 2), ready)
                    if n is not None and j == tiles - 1:
                        norm_squares(n, range(KT // 2, KT), ready)
                        norm_root(n)
                    if b.m0 + j + 2 < MAINS:
                        hi(b, j + 2, 0)

            act.wait_ge(dec_abs, 1)
            nc.scalar.activation(small[:, 8:16], small[:, 0:8], ACT.Exp, scale=-1.0).then_inc(dec_e, 1)
            act.wait_ge(dec_w, 1)
            nc.scalar.activation(small[:, 24:32], small[:, 16:24], ACT.Ln).then_inc(dec_ln, 1)

            act.wait_ge(x_in, 16)
            act.wait_ge(eps_set, 1)
            norm_squares(0, range(KT), lambda k: None)
            norm_root(0)


            b0 = SEG["ret0"]
            hi(b0, 0, 0)
            hi(b0, 1, 0)
            act.dma_start(dm[:], dr["diff"]).then_inc(dec_in, 16)
            act.dma_start(iota, dr["iota"]).then_inc(dec_in, 16)
            act.dma_start(tri, dr["tri"]).then_inc(dec_in, 16)
            act.dma_start(rope_t[:], dr["rope_t"]).then_inc(rope_in, 16)
            norm_hi(0)

            act.wait_ge(dec_lg, 1)
            act.wait_ge(dec_in, 48)
            act.wait_ge(const_in, 16)
            for d in range(2):
                for h in range(HEADS):
                    lg = small[:, 40 + 4 * d + h:41 + 4 * d + h]
                    nc.scalar.activation(dm[:, d, h, :], dm[:, d, h, :], ACT.Exp, scale=lg)
                    nc.scalar.activation(xi[:, d, h, :], iota[:, d, :], ACT.Exp, scale=lg)
                    nc.scalar.activation(small[:, 48 + 4 * d + h:49 + 4 * d + h],
                                         cst[:, C_ZF + d:C_ZF + d + 1], ACT.Exp, scale=lg)
            nc.scalar.activation(small[:, 56:64], small[:, 40:48], ACT.Exp, scale=float(P)).then_inc(dec_exp, 1)
            zeta = small[:, 48:56].rearrange("p (d h) -> p d h", d=2)

            def head(b, h, first_head):
                for j in range(4):
                    act.wait_ge(chunk_done, b.done(j, h))
                    hi(b, j + 2, h)
                    bank, scale = 2 * (j % 2), 1.0 if j < 2 else DK ** -0.5
                    ctx_to = (qT if j < 2 else kT)[:, j % 2, 0:NCTX]
                    lat = front[:, j * NLAT:(j + 1) * NLAT]
                    nc.scalar.activation(ctx_to, ps[:, bank, 0:NCTX], ACT.Copy, scale=scale)
                    nc.scalar.activation(lat[:, 0:CUT], ps[:, bank, NCTX:HALF], ACT.Copy, scale=scale)
                    nc.scalar.activation(lat[:, CUT:NLAT], ps[:, bank + 1, 0:HALF], ACT.Copy,
                                         scale=scale).then_inc(qk_evac, 1)
                    if j == 0:
                        act.dma_start(S[:], dr["state"][h]).then_inc(S_in, 16)
                    if not first_head and j in (1, 2):
                        turn_y(h - 1, (0, 1, 2) if j == 1 else (3, 4))
                j = 4
                if not first_head:
                    for k in range(4):
                        hi(b, 4 + k + 2, h)
                    j = 8
                for proj in range(3):
                    for kc in range(3):
                        hi(b, j + kc + 2, h)
                    for t in range(TT):
                        if t == TT - 1:
                            act.wait_ge(chunk_done, b.done(j + 3, h))
                        else:
                            act.wait_ge(tile_done, 12 * h + 4 * proj + t + 1)
                        if proj == 0:
                            if t == 0:
                                act.wait_ge(rope_done, 2 * h + 2)
                            op = nc.scalar.copy(v[:, t, :], ps[:, t, :])
                        else:
                            op = nc.scalar.activation((gf, gb)[proj - 1][:, t, :], ps[:, t, :], ACT.Silu)
                        op.then_inc(tok_evac, 1)
                    hi(b, j + 3 + 2, h)
                    j += 4
                    if proj == 0:
                        act.wait_ge(scores_done, h + 1)
                        if first_head:
                            act.wait_ge(dec_ready, 1)
                        zf, zb = zeta[:, 0, bass.ds(h, 1)], zeta[:, 1, bass.ds(h, 1)]
                        pair = lambda bank: ps[:, bank, :].rearrange("p (c d) -> p c d", c=2)
                        nc.scalar.activation(kz[:, 0, 0, :], ps[:, 6, P:P + DK], ACT.Copy, scale=zf)
                        nc.scalar.activation(kz[:, 1, 0, :], ps[:, 6, P:P + DK], ACT.Copy, scale=zb)
                        nc.scalar.activation(kz[:, 0, 1:3, :], pair(7), ACT.Copy, scale=zf)
                        nc.scalar.activation(kz[:, 1, 1, :], ps[:, 7, DK:2 * DK], ACT.Copy, scale=zb)
                        nc.scalar.activation(kz[:, 0, 3, :], ps[:, 4, 0:DK], ACT.Copy, scale=zf)
                        nc.scalar.activation(kz[:, 1, 2:4, :], pair(4), ACT.Copy, scale=zb).then_inc(kz_done, 1)
                for n in range(10):
                    act.drain()
                    act.wait_ge(o_done, 10 * h + n + 1)
                    nc.scalar.activation(junk[:], ps[:, 6 + n % 2, :], ACT.Square,
                                         accum_out=small[:, 64 + n:65 + n]).then_inc(ss_done, 1)
                    if n == 1:
                        if not first_head:
                            act.wait_ge(st_stored, 32 * h)
                        for d in range(2):
                            act.wait_ge(u_done, 8 * h + d + 1)
                            nc.scalar.copy(st_out[:, d], ps[:, 2 * d:2 * d + 2, :]).then_inc(st_copied, 1)
                        for d in range(2):
                            act.wait_ge(st_copied, 2 * h + d + 1)
                            act.dma_start(dr["new_state"][d, h], st_out[:, d]).then_inc(st_stored, 16)

            def turn_y(h, ns):
                for n in ns:
                    t = Y_ORDER[n]
                    act.wait_ge(yT_done, TT * h + n + 1)
                    nc.scalar.copy(y_h[:, :, t * P:(t + 1) * P],
                                   ps[:, 5 + n % 3, :].rearrange("p (k q) -> p k q", k=4)).then_inc(yhi_done, 1)

            head(b0, 0, True)
            with act.Fori(1, HEADS) as h:
                head(SEG["ret"], h, False)
            turn_y(HEADS - 1, range(TT))

            def after_out(o):
                return lambda k: act.wait_ge(res_done, 16 * o + max(2 * k + 2, 8))

            def ffn_open(l):
                for w in range(2):
                    nc.scalar.activation(small[:, 80 + w:81 + w], eps, ACT.Silu).then_inc(a_evac[l], 1)

            def ffn_phase(l, norm):
                tiles0 = 0
                for g, tiles in enumerate(GROUPS):
                    b = SEG["in", l, g]
                    pairs = b.mains // 2
                    with act.Fori(0, tiles // pairs) as i:
                        for q in range(pairs):
                            n = tiles0 + q
                            par = q % 2
                            blk = ada_at(b, g, q, i)
                            for w in range(2):
                                act.wait_ge(chunk_done, b.done(2 * q + w, i))
                                hi(b, 2 * q + w + 2, i)
                                act.wait_ge(conv_done[l], 2 * n + w + 1 + 2 * pairs * i)
                                a = ca[:, par, w]
                                nc.scalar.copy(a[:, 1:1 + NCTX], ps[:, 2 * w, 0:NCTX])
                                nc.scalar.copy(a[:, NCTX + 2:NCTX + 2 + CUT], ps[:, 2 * w, NCTX:HALF])
                                nc.scalar.copy(a[:, NCTX + 2 + CUT:NCTX + 2 + NLAT],
                                               ps[:, 2 * w + 1, 0:HALF]).then_inc(a_evac[l], 1)
                                if blk is not None and w == 0:
                                    slot, used = b.chunk(b.ada[(4 * q if g == 0 else 0) + 3], i)
                                    act.wait_ge(raw_used[slot], used)
                                    nc.scalar.copy(ada_o[:, q, :], ps[:, 4 + q, :]).then_inc(ada_copied, 1)
                            act.wait_ge(conv_done[l], 4 + 2 * n + 2 + 2 * pairs * i)
                            nc.scalar.activation(sg[:, par, 0:CONV], cc[:, par, 1, 0:CONV],
                                                 ACT.Silu).then_inc(silu_done[l], 1)
                            act.wait_ge(md_done[l], n + 1 + pairs * i)
                            nc.scalar.copy(m_h[:, pairs * i + q, :], md[:, par, :]).then_inc(mhi_done[l], 1)
                    last = g == len(GROUPS) - 1
                    out_act(SEG["out", l, g], tiles, norm if last else None, after_out(4 * (l + 1) + g))
                    tiles0 += tiles

            out_act(SEG["wo3"], 4, 1, after_out(3))
            ffn_open(0)
            norm_hi(1)
            ffn_phase(0, 2)
            act.wait_ge(at_zero, 1)
            act.dma_start(rope_a[:], dr["rope_a"]).then_inc(at_in, 16)
            act.dma_start(maskf[:], dr["mask"]).then_inc(at_in, 16)
            act.dma_start(cv[:], dr["cache_v"]).then_inc(at_in, 16)
            for kv in range(KVH):
                rows = slice(64 * (kv % 2), 64 * (kv % 2) + 64)
                act.dma_start(ck[rows, kv, :], dr["cache_k"][kv]).then_inc(at_in, 16)
            norm_hi(2)

            b = SEG["att"]
            for j in range(10):
                act.wait_ge(chunk_done, b.done(j, 0))
                hi(b, j + 2, 0)
                bank = 2 * (j % 2)
                if j >= 4:
                    act.wait_ge(arope_done, j - 3)
                if j == 0:
                    for k in POOL_LO[-1], KT - 1:
                        wait_rest(act, 2, k)
                if j < 8:
                    nc.scalar.copy(aq[:, j, 0:NCTX], ps[:, bank, 0:NCTX])
                else:
                    for r in range(2):
                        rows = slice(64 * r, 64 * r + 64)
                        nc.scalar.copy(ak[rows, 2 * (j - 8) + r, 0:NCTX], ps[rows, bank, 0:NCTX])
                nc.scalar.copy(lat_in[:, j % 4, 0:CUT], ps[:, bank, NCTX:HALF])
                nc.scalar.copy(lat_in[:, j % 4, CUT:NLAT], ps[:, bank + 1, 0:HALF]).then_inc(aqk_evac, 1)
            hi(b, 12, 0)
            for t in range(TT):
                if t == TT - 1:
                    act.wait_ge(chunk_done, b.done(11, 0))
                else:
                    act.wait_ge(atile_done, t + 1)
                nc.scalar.copy(av[:, t, :], ps[:, (4 + t) % 8, 0:KVH * HD]).then_inc(av_evac, 1)
            hi(b, 13, 0)
            act.wait_ge(aqk_evac, 10)
            act.wait_ge(av_evac, 1)
            for kv in range(KVH):
                rows = slice(64 * (kv % 2), 64 * (kv % 2) + 64)
                act.dma_start(dr["new_k"][kv], ak[rows, kv, 0:NCTX]).then_inc(kv_stored, 16)
            act.dma_start(dr["new_v"], av[:, 0, :]).then_inc(kv_stored, 16)

            stat = small[:, 0:64].rearrange("p (a b) -> p a b", b=4)

            def unit_exp(u, half):
                w, st = P * len(key_blocks(u // KVH)), 8 * (u % 2)
                act.wait_ge(am_done, 4 * u + 2 * half + 2)
                if u >= 2 and half == 0:
                    act.wait_ge(apv_done, u - 1)
                for g in (2 * half, 2 * half + 1):
                    op = nc.scalar.activation(pr[:, u % 2, g, 0:w], ps[:, g, 0:w], ACT.Exp, scale=HD ** -0.5,
                                              bias=stat[:, st + 1, g:g + 1], accum_out=stat[:, st + 3, g:g + 1])
                if half == 1:
                    op = nc.scalar.activation(stat[:, st + 4, :], stat[:, st + 2, :], ACT.Exp)
                op.then_inc(ae_done, 1)

            for u in range(UNITS + 1):
                if u < UNITS:
                    unit_exp(u, 0)
                if u >= 1:
                    for kb in PT_ACT:
                        if kb < len(key_blocks((u - 1) // KVH)):
                            x = PT_AT[u - 1] + kb
                            act.wait_ge(apt_done, x + 1)
                            if u >= 3:
                                act.wait_ge(apv_done, u - 2)
                            nc.scalar.copy(pT[:, (u - 1) % 2, kb, :], ps[:, 4 + x % 3, :]).then_inc(apt_act, 1)
                if u < UNITS:
                    unit_exp(u, 1)
                if u >= 2 and u % 2 == 0:
                    act.wait_ge(apv_done, u)
                    o, n = (u - 1) // 2, (u - 1) // KVH
                    nc.scalar.copy(h_h[:, (o % 2) * G:(o % 2) * G + G, tok_of(n)],
                                   ps[:, 7, :].rearrange("p (g q) -> p g q", g=G)).then_inc(aohi_done, 1)
            out_act(SEG["att_o"], KT, 3, after_out(7))
            ffn_open(1)
            norm_hi(3)
            ffn_phase(1, 4)
            for k in range(KT):
                act.wait_ge(hf_done, KT * 4 + k + 1)
                act.dma_start(dr["y"][k], aq[:, k, :]).then_inc(y_stored, 16)

        @block.gpsimd
        def _(pool):
            def lo(b, j, i):
                s, _ = b.chunk(b.at[j], i)
                r, n = b.split(j, i)
                pool.wait_ge(hi_ready[r], n)
                nc.gpsimd.tensor_tensor(w_l[:, r, :], raw[:, s, :], w_h[:, r, :].bitcast(F32),
                                        ALU.subtract).then_inc(raw_used[s], 1)

            nc.gpsimd.memset(small[:, 95:96], EPS).then_inc(eps_set, 1)
            nc.gpsimd.memset(csil[:], 0.0).then_inc(csil_zero, 1)
            nc.gpsimd.memset(small[:, 84:85], -0.5)
            nc.gpsimd.memset(small[:, 85:86], 1.0 / DV)
            pool.drain()

            def rms(h):
                for n in range(10):
                    pool.wait_ge(ss_done, 10 * h + n + 1)
                    out = small[:, 74 + n:75 + n]
                    nc.gpsimd.tensor_tensor(out, small[:, 64 + n:65 + n], small[:, 85:86], ALU.mult)
                    pool.drain()
                    nc.gpsimd.tensor_tensor(out, out, eps, ALU.add)
                    pool.drain()
                    nc.gpsimd.tensor_tensor(out, out, small[:, 84:85], ALU.pow).then_inc(rms_done, 1)

            def norm_add(n, ks):
                for k in ks:
                    pool.wait_ge(sq_done, KT * n + k + 1)
                    nc.gpsimd.tensor_tensor(sq_sum, sq[:, 0] if k == 1 else sq_sum, sq[:, k % 2],
                                            ALU.add).then_inc(sq_added, 1)
                    pool.drain()

            def norm_rest(n):
                for k in POOL_LO:
                    pool.wait_ge(hhi_done, KT * n + k + 1)
                    nc.gpsimd.tensor_tensor(h_l[:, k, :], hf[:, k % 4, :], h_h[:, k, :].bitcast(F32),
                                            ALU.subtract).then_inc(hlo_pool, 1)

            def out_pool(b, tiles, n):
                for j in range(tiles):
                    if n is not None and j == tiles - 2:
                        norm_add(n, range(1, KT // 2))
                    if n is not None and j == tiles - 1:
                        norm_add(n, range(KT // 2, KT - 2))
                    if b.m0 + j + 2 < MAINS:
                        lo(b, j + 2, 0)

            norm_add(0, range(1, KT - 2))
            for j in range(2):
                lo(SEG["ret0"], j, 0)
            norm_rest(0)
            for j in range(16):
                lo(SEG["ret0"], j + 2, 0)
            rms(0)
            with pool.Fori(1, HEADS) as h:
                for j in range(20):
                    lo(SEG["ret"], j + 2, h)
                rms(h)
            out_pool(SEG["wo3"], 4, 1)
            norm_rest(1)
            for l in range(2):
                for g, tiles in enumerate(GROUPS):
                    b = SEG["in", l, g]
                    with pool.Fori(0, 2 * tiles // b.mains) as i:
                        for j in range(b.mains):
                            lo(b, j + 2, i)
                    last = g == len(GROUPS) - 1
                    out_pool(SEG["out", l, g], tiles, 2 + 2 * l if last else None)
                if l == 0:
                    pool.wait_ge(res_done, 16 * 7)
                    nc.gpsimd.memset(ak[:], 0.0)
                    nc.gpsimd.memset(ck[:], 0.0)
                    pool.drain()
                    nc.gpsimd.memset(small[:, 94:95], 0.0).then_inc(at_zero, 1)
                    norm_rest(2)
                    for j in range(12):
                        lo(SEG["att"], j + 2, 0)
                    out_pool(SEG["att_o"], KT, 3)
                    norm_rest(3)

        @block.vector
        def _(dve):
            V = nc.vector

            def norm_diag(n):
                dve.wait_ge(root_done, n + 1)
                V.reciprocal(r_rms, root)
                dve.drain()
                for t in range(TT):
                    V.tensor_scalar(diag[:, t], ident, r_rms[:, t:t + 1], None, ALU.mult).then_inc(diag_done, 1)

            def norm_dve(n, l, shift, scale):
                if n < 4:
                    for s in range(2):
                        V.scalar_tensor_tensor(out=mod_a[:, :, s], in0=mods[:, l, 8 * scale:8 * scale + 8, s], scalar=1.0,
                                               in1=norm_g[:, n, :], op0=ALU.add, op1=ALU.mult)
                dve.wait_ge(rstd_done, TT * (n + 1))
                dve.drain()
                if n == 4:
                    for k in range(KT):
                        V.scalar_tensor_tensor(out=aq[:, k, :], in0=xT[:, k, :], scalar=norm_g[:, 4, k:k + 1],
                                               in1=rstd, op0=ALU.mult, op1=ALU.mult).then_inc(hf_done, 1)
                    return
                for k in range(KT + 1):
                    if k < KT:
                        V.tensor_tensor(xn[:, k % 2, :], xT[:, k, :], rstd, ALU.mult)
                        dve.drain()
                        if k >= 4:
                            wait_rest(dve, n, k - 4)
                        for s, tok in ((1, slice(0, NCTX)), (0, slice(NCTX, T))):
                            op = V.tensor_scalar(hf[:, k % 4, tok], xn[:, k % 2, tok], mod_a[:, k, s:s + 1],
                                                 mods[:, l, 8 * shift + k, s:s + 1], ALU.mult, ALU.add)
                        op.then_inc(hf_done, 1)
                    if k >= 1 and k - 1 not in POOL_LO:
                        dve.wait_ge(hhi_done, KT * n + k)
                        V.tensor_tensor(h_l[:, k - 1, :], hf[:, (k - 1) % 4, :], h_h[:, k - 1, :].bitcast(F32),
                                        ALU.subtract).then_inc(hlo_dve, 1)

            def ada_copy(b, k0, i, par):
                s, n = b.chunk(b.ada[k0 + 3], i)
                dve.wait_ge(raw_used[s], n)
                V.tensor_copy(ada_o[:, par, :], ps[:, 4 + par, :]).then_inc(ada_copied, 1)

            def ada_mods(par, turned, l, blk):
                dve.wait_ge(ada_turned, turned)
                got = ps[:, 4 + par, 0:8].rearrange("p (f s) -> p f s", s=2)
                m5 = mods[:, l].rearrange("p (b f) s -> p b f s", f=4)
                b5 = ada_b[:, l].rearrange("p (b f) -> p b f", f=4)
                for s in range(2):
                    op = V.tensor_tensor(m5[:, blk, :, s], got[:, :, s], b5[:, blk, :], ALU.add)
                op.then_inc(mods_done, 1)

            def residual(o, b, j0, i, tiles, l, gate):
                for mh in range(2):
                    for at in range(8):
                        bank = out_bank(mh, at)
                        if at < 7:
                            dve.wait_ge(out_done, 14 * o + 7 * mh + at + 1)
                        else:
                            dve.wait_ge(chunk_done, b.done(j0 + (mh + 1) * tiles // 2 - 1, i))
                        m = 4 * mh + bank // 2
                        for cols, tok, s in spans(bank % 2):
                            op = V.scalar_tensor_tensor(out=xT[:, m, tok], in0=ps[:, bank, cols],
                                                        scalar=mods[:, l, 8 * gate + m, s:s + 1],
                                                        in1=xT[:, m, tok], op0=ALU.mult, op1=ALU.add)
                        op.then_inc(res_done, 1)

            x, ab, e, w, ln, ra, lg = (vec[:, V_DEC:V_DEC + 8], *(small[:, 8 * n:8 * n + 8] for n in (0, 1, 2, 3, 4, 5)))
            t1, t2 = small[:, 64:72], small[:, 72:80]
            dve.wait_ge(vec_in, 16)
            V.tensor_scalar(t1, x, -1.0, None, ALU.mult)
            dve.drain()
            V.tensor_tensor(ab, x, t1, ALU.max).then_inc(dec_abs, 1)
            dve.wait_ge(dec_e, 1)
            V.tensor_scalar(w, e, 1.0, None, ALU.add).then_inc(dec_w, 1)
            dve.drain()
            V.tensor_scalar(t1, w, -1.0, 1e-30, ALU.add, ALU.max)
            dve.drain()
            V.reciprocal(t2, t1)
            dve.drain()
            V.tensor_tensor(ra, t2, e, ALU.mult)
            dve.drain()
            dve.wait_ge(dec_ln, 1)
            V.tensor_tensor(t1, ln, ra, ALU.mult)
            dve.drain()
            V.scalar_tensor_tensor(out=lg, in0=x, scalar=0.0, in1=t1, op0=ALU.min,
                                   op1=ALU.subtract).then_inc(dec_lg, 1)
            first = Body(0, 0, "a" * 16)
            for blk in range(4):
                ada_copy(first, 4 * blk, 0, blk % 2)
                ada_mods(blk % 2, blk + 1, 0, blk)
                if blk == 2:
                    dve.wait_ge(const_in, 16)
                    norm_diag(0)
            dve.drain()
            norm_dve(0, 0, 0, 1)
            dve.wait_ge(dec_exp, 1)
            for d in range(2):
                op = V.tensor_tensor(dm[:, d], dm[:, d], over(tri[:, d, :], HEADS), ALU.mult)
            op.then_inc(dec_ready, 1)
            gch = small[:, 56:64].rearrange("p (d h) -> p d h", d=2)

            def rope(dst, a, b, p1, p2):
                cos, sin = rope_t[:, 0], rope_t[:, 1]
                V.tensor_tensor(p1, a, cos, ALU.mult)
                V.tensor_tensor(p2, b, sin, ALU.mult)
                dve.drain()
                V.tensor_tensor(dst[:, 0, NCTX:T], p1, p2, ALU.subtract)
                dve.drain()
                V.tensor_tensor(p1, a, sin, ALU.mult)
                V.tensor_tensor(p2, b, cos, ALU.mult)
                dve.drain()
                V.tensor_tensor(dst[:, 1, NCTX:T], p1, p2, ALU.add).then_inc(rope_done, 1)
                dve.drain()

            def head(b, h, first_head):
                if first_head:
                    dve.wait_ge(rope_in, 16)
                lat = front[:, 0:4 * NLAT].rearrange("p (j t) -> p j t", j=4)
                ada_copy(b, 0, h, 0)
                ada_mods(0, 4 + 2 * h + 1, 0, 4 + 2 * h)
                for n, dst in enumerate((qT, kT)):
                    if n == 1 and not first_head:
                        turn_y(h - 1)
                    dve.wait_ge(qk_evac, 4 * h + 2 * n + 2)
                    rope(dst, lat[:, 2 * n], lat[:, 2 * n + 1], front[:, 4 * NLAT:5 * NLAT], gb[:, 0, :])
                if not first_head:
                    residual(h - 1, b, 4, h, 4, 0, 2)
                ada_copy(b, 4, h, 1)
                ada_mods(1, 4 + 2 * h + 2, 0, 4 + 2 * h + 1)
                dve.wait_ge(scores_done, h + 1)
                for d in range(2):
                    V.tensor_tensor(kT[:, d, 0:P], ps[:, 3, 0:P], dm[:, d, h, :], ALU.mult)
                    op = V.tensor_tensor(kT[:, d, NCTX:T].rearrange("p (c i) -> p c i", c=4),
                                    ps[:, 5, :].rearrange("p (c i) -> p c i", c=4), over(dm[:, d, h, :], 4), ALU.mult)
                op.then_inc(scores_read, 1)
                for d in (0, 1):
                    for t in range(2):
                        src = qT[:, t, NCTX:T].rearrange("p (c i) -> p c i", c=4)
                        dst = src if d == 1 else qf[:, t, :].rearrange("p (c i) -> p c i", c=4)
                        op = V.tensor_tensor(dst, src, over(xi[:, d, h, :], 4), ALU.mult)
                    if d == 0:
                        dve.drain()
                op.then_inc(sT_done, 1)
                dve.wait_ge(tok_evac, 15 * h + 15)
                for n in range(10):
                    s, d = (n - 2) // 2, n % 2
                    t = 0 if n < 2 else 1 + (s if d == 0 else 3 - s)
                    if 2 <= n < 8:
                        dve.wait_ge(u_done, 8 * h + n + 1)
                        V.scalar_tensor_tensor(out=S[:, d], in0=S[:, d], scalar=gch[:, d, bass.ds(h, 1)],
                                               in1=ps[:, 2 * d:2 * d + 2, :], op0=ALU.mult,
                                               op1=ALU.add).then_inc(S_upd, 1)
                    dve.wait_ge(rms_done, 10 * h + n + 1)
                    g = (gf, gb)[d]
                    V.scalar_tensor_tensor(out=g[:, t, :], in0=ps[:, 6 + d, :], scalar=small[:, 74 + n:75 + n],
                                           in1=g[:, t, :], op0=ALU.mult, op1=ALU.mult).then_inc(o_evac, 1)
                    if n == 1 or n >= 6:
                        dve.drain()
                        V.tensor_tensor(gf[:, t, :], gf[:, t, :], gb[:, t, :], ALU.add).then_inc(y_done, 1)
                dve.drain()

            def turn_y(h):
                for n, t in enumerate(Y_ORDER):
                    dve.wait_ge(yhi_done, TT * h + n + 1)
                    cols = slice(t * P, (t + 1) * P)
                    V.tensor_tensor(y_l[:, :, cols], ps[:, 5 + n % 3, :].rearrange("p (k q) -> p k q", k=4),
                                    y_h[:, :, cols].bitcast(F32), ALU.subtract).then_inc(ylo_done, 1)

            head(SEG["ret0"], 0, True)
            with dve.Fori(1, HEADS) as h:
                head(SEG["ret"], h, False)
            turn_y(HEADS - 1)
            residual(3, SEG["wo3"], 0, 0, 4, 0, 2)

            def ffn_phase(l, o0):
                for par in range(2):
                    for w in range(2):
                        V.memset(ca[:, par, w], 0.0).then_inc(conv_done[l], 1)
                tiles0 = 0
                for g, tiles in enumerate(GROUPS):
                    b = SEG["in", l, g]
                    pairs = b.mains // 2
                    with dve.Fori(0, tiles // pairs) as i:
                        for q in range(pairs):
                            n, par = tiles0 + q, q % 2
                            blk = ada_at(b, g, q, i)
                            for w in range(2):
                                if blk is not None and w == 1:
                                    ada_mods(q, blk + 1, 1, blk - 12)
                                dve.wait_ge(a_evac[l], 2 + 2 * n + w + 1 + 2 * pairs * i)
                                a, c = ca[:, par, w], cc[:, par, w, 0:CONV]
                                tap = [conv_w[:, l, w * FT + n + pairs * i, k:k + 1] for k in range(4)]
                                V.tensor_scalar(c, a[:, 1:1 + CONV], tap[1], tap[3], ALU.mult, ALU.add)
                                dve.drain()
                                V.scalar_tensor_tensor(out=c, in0=a[:, 0:CONV], scalar=tap[0], in1=c,
                                                       op0=ALU.mult, op1=ALU.add)
                                dve.drain()
                                V.scalar_tensor_tensor(out=c, in0=a[:, 2:2 + CONV], scalar=tap[2], in1=c,
                                                       op0=ALU.mult, op1=ALU.add).then_inc(conv_done[l], 1)
                            dve.drain()
                            dve.wait_ge(silu_done[l], n + 1 + pairs * i)
                            V.tensor_tensor(md[:, par, 0:NCTX], sg[:, par, 0:NCTX], cc[:, par, 0, 0:NCTX], ALU.mult)
                            V.tensor_tensor(md[:, par, NCTX:T], sg[:, par, LAT_AT:CONV], cc[:, par, 0, LAT_AT:CONV],
                                            ALU.mult).then_inc(md_done[l], 1)
                            dve.wait_ge(mhi_done[l], n + 1 + pairs * i)
                            V.tensor_tensor(m_l[:, pairs * i + q, :], md[:, par, :],
                                            m_h[:, pairs * i + q, :].bitcast(F32),
                                            ALU.subtract).then_inc(mlo_done[l], 1)
                    tiles0 += tiles
                    residual(o0 + g, SEG["out", l, g], 0, 0, tiles, l, 5)
                dve.drain()

            dve.drain()
            norm_diag(1)
            norm_dve(1, 0, 3, 4)
            dve.wait_ge(st_stored, 32 * HEADS)
            ffn_phase(0, 4)
            norm_diag(2)
            norm_dve(2, 1, 0, 1)

            dve.wait_ge(at_in, 16 * AT_LOADS)
            V.tensor_copy(maskb[:], maskf[:])
            V.tensor_copy(identb[:], ident).then_inc(at_bf, 1)
            for j in range(10):
                dve.wait_ge(aqk_evac, j + 1)
                lat = lat_in[:, j % 4]
                V.stream_shuffle(swapped, lat, [(x + 16) % 32 for x in range(32)])
                V.tensor_tensor(r1, lat, rope_a[:, 0], ALU.mult)
                dve.drain()
                V.tensor_tensor(r2, swapped, rope_a[:, 1], ALU.mult)
                dve.drain()
                if j < 8:
                    op = V.tensor_tensor(aq[:, j, NCTX:T], r1, r2, ALU.add)
                else:
                    for r in range(2):
                        rows = slice(64 * r, 64 * r + 64)
                        op = V.tensor_tensor(ak[rows, 2 * (j - 8) + r, NCTX:T], r1[rows], r2[rows], ALU.add)
                op.then_inc(arope_done, 1)
                dve.drain()

            stat = small[:, 0:64].rearrange("p (a b) -> p a b", b=4)

            def unit_max(u, half):
                n, kv = divmod(u, KVH)
                w, st = P * len(key_blocks(n)), 8 * (u % 2)
                gs = slice(2 * half, 2 * half + 2)
                sink = vec[:, V_SINK + kv * G:V_SINK + (kv + 1) * G][:, gs]
                dve.wait_ge(as_done, 2 * u + half + 1)
                V.tensor_reduce(stat[:, st, gs], ps[:, gs, 0:w], AX.X, ALU.max)
                dve.drain()
                V.scalar_tensor_tensor(out=stat[:, st + 6, gs], in0=stat[:, st, gs], scalar=HD ** -0.5, in1=sink,
                                       op0=ALU.mult, op1=ALU.max)
                dve.drain()
                V.tensor_scalar(stat[:, st + 1, gs], stat[:, st + 6, gs], -1.0, None, ALU.mult).then_inc(am_done, 1)
                V.tensor_tensor(stat[:, st + 2, gs], sink, stat[:, st + 6, gs], ALU.subtract).then_inc(am_done, 1)

            def unit_norm(u):
                w, st = P * len(key_blocks(u // KVH)), 8 * (u % 2)
                dve.wait_ge(ae_done, 2 * u + 2)
                V.tensor_tensor(stat[:, st + 5, :], stat[:, st + 3, :], stat[:, st + 4, :], ALU.add)
                dve.drain()
                V.reciprocal(stat[:, st + 7, :], stat[:, st + 5, :])
                dve.drain()
                for g in range(G):
                    p = pr[:, u % 2, g, 0:w]
                    op = V.tensor_scalar(p, p, stat[:, st + 7, g:g + 1], None, ALU.mult)
                op.then_inc(ap_done, 1)

            def unit_pt(u, kb):
                if kb in PT_ACT or kb >= len(key_blocks(u // KVH)):
                    return
                x = PT_AT[u] + kb
                dve.wait_ge(apt_done, x + 1)
                if u >= 2:
                    dve.wait_ge(apv_done, u - 1)
                V.tensor_copy(pT[:, u % 2, kb, :], ps[:, 4 + x % 3, :]).then_inc(apt_dve, 1)

            def pair_rest(o):
                dve.wait_ge(aohi_done, o + 1)
                at = slice((o % 2) * G, (o % 2) * G + G)
                tok = tok_of(2 * o // KVH)
                V.tensor_tensor(h_l[:, at, tok], ps[:, 7, :].rearrange("p (g q) -> p g q", g=G),
                                h_h[:, at, tok].bitcast(F32), ALU.subtract).then_inc(aolo_done, 1)

            for half in range(2):
                unit_max(0, half)
            for u in range(UNITS):
                unit_norm(u)
                if u >= 2 and u % 2 == 0:
                    pair_rest(u // 2 - 1)
                if u + 1 < UNITS:
                    unit_max(u + 1, 0)
                unit_pt(u, 0)
                if u + 1 < UNITS:
                    unit_max(u + 1, 1)
                unit_pt(u, 3)
            pair_rest(UNITS // 2 - 1)
            residual(7, SEG["att_o"], 0, 0, KT, 1, 2)
            dve.drain()
            norm_diag(3)
            norm_dve(3, 1, 3, 4)
            dve.wait_ge(kv_stored, 16 * 5)
            ffn_phase(1, 8)
            norm_diag(4)
            norm_dve(4, 1, 0, 0)


def _layout(x):
    import numpy as np
    f = np.float32
    a = {k: np.asarray(v) for k, v in x.items()}

    def feature(w):
        k, m = w.shape
        return w.reshape(k // P, P, m // P, P).transpose(2, 1, 0, 3).reshape(m // P, P, -1)

    def token(w):
        k, n = w.shape
        return w.reshape(k // 256, 2, P, n // 512, 512).transpose(3, 0, 2, 1, 4).reshape(-1, P, CH)

    dims = np.concatenate([np.arange(64), np.arange(128, 192), np.arange(64, 128), np.arange(192, 256)])
    ada0, ada1 = token(a["ada_w"][0]), token(a["ada_w"][1])
    parts = [ada0[0:16]]
    wo = token(a["ret_wo"][0])
    wo = wo.reshape(2, HEADS, 2, P, CH)
    for h in range(HEADS):
        q = feature(a["ret_wq"][0][:, h * DK + dims])
        k = feature(a["ret_wk"][0][:, h * DK + dims])
        parts += [q, ada0[16 + 8 * h:20 + 8 * h], k]
        if h:
            parts.append(wo[:, h - 1].reshape(4, P, CH))
        wv = token(a["ret_wv"][0][:, h * DV:(h + 1) * DV])
        parts += [wv[0:1], ada0[20 + 8 * h:24 + 8 * h], wv[1:]]
        for w in ("ret_wg_fwd", "ret_wg_bwd"):
            parts.append(token(a[w][0][:, h * DV:(h + 1) * DV]))
    parts.append(wo[:, 3].reshape(4, P, CH))
    heads = [np.concatenate([np.arange(HD) + (kv * G + g) * HD for kv in (2 * p, 2 * p + 1)])
             for p in range(2) for g in range(G)]
    heads = np.concatenate(heads)
    for l in range(2):
        w_in = feature(a["ffn_w_in"][l])
        w_out = token(a["ffn_w_out"][l]).reshape(2, FT // 2, P, CH)
        t0 = 0
        ada = 0
        for g, tiles in enumerate(GROUPS):
            b = SEG["in", l, g]
            pairs = b.mains // 2
            for i in range(tiles // pairs):
                for q in range(pairs):
                    t = t0 + i * pairs + q
                    parts.append(w_in[[t, FT + t]])
                    if b.kinds[b.at[2 * q + 1] + 1:].startswith("a"):
                        parts.append(ada1[ada:ada + 4])
                        ada += 4
            parts.append(w_out[:, t0 // 2:(t0 + tiles) // 2].reshape(-1, P, CH))
            t0 += tiles
        if l == 0:
            parts.append(feature(a["attn_wq"][0][:, heads]))
            parts.append(feature(a["attn_wk"][0]))
            parts.append(a["attn_wv"][0].reshape(2, 4, P, KVH * HD).transpose(0, 2, 1, 3).reshape(2, P, CH))
            parts.append(token(a["attn_wo"][0][heads]))
    stream = np.concatenate(parts)
    assert stream.shape == (CHUNKS, P, CH), stream.shape

    vec = np.zeros((P, V_W), f)
    vec[:, V_C:V_C + 16] = np.stack([a["c"][0], a["c_ctx"]]).reshape(2, KT, P).transpose(2, 1, 0).reshape(P, 16)
    vec[:, V_ADAB:V_ADAB + 96] = a["ada_b"].reshape(2 * 48, P).T
    norms = [a["norm_mix"][0], a["norm_ffn"][0], a["norm_mix"][1], a["norm_ffn"][1], a["norm_final"]]
    vec[:, V_NORM:V_NORM + 40] = np.stack(norms).reshape(40, P).T
    vec[:, V_DEC:V_DEC + 4] = a["ret_decay_fwd"]
    vec[:, V_DEC + 4:V_DEC + 8] = a["ret_decay_bwd"]
    vec[:, V_SINK:V_SINK + QH] = a["attn_sink"]
    taps = np.concatenate([a["ffn_conv_w"], a["ffn_conv_b"][:, None]], axis=1)
    vec[:, V_CONV:] = taps.reshape(2, 4, 2 * FT, P).transpose(3, 0, 2, 1).reshape(P, -1)

    i = np.arange(P)
    cst = np.zeros((P, C_W), f)
    cst[:, C_ID:C_ID + P] = np.eye(P)
    cst[:, C_ONE:C_ONE + P] = 1
    for g in range(4):
        for s in range(2):
            cst[32 * g + s, C_SEL + s] = 1
    cst[:, C_ZF], cst[:, C_ZB] = P - 1 - i, i
    d = i[None, :] - i[:, None]
    diff = np.stack([np.maximum(d, 0), np.maximum(-d, 0)], 1).astype(f)
    tri = np.stack([d >= 0, d <= 0], 1).astype(f)
    iota = np.broadcast_to(np.stack([i + 1, P - i]), (P, 2, P)).astype(f)
    mask = np.stack([np.where(d >= 0, 0, NEG), np.where(d <= 0, 0, NEG)], 1).astype(f)
    t = np.arange(NLAT)
    rows, cols = (t // 64).astype(f), (t % 64).astype(f)

    def table(freq, is_row, n, sign):
        inv = (f(10000.0) ** (-np.arange(n, dtype=f) / f(n))).astype(f)
        pos = np.where(is_row[:, None], rows[None], cols[None]).astype(f)
        ang = (pos * inv[freq][:, None]).astype(f)
        return np.stack([np.cos(ang), np.sin(ang) * sign[:, None]], 1).astype(f)

    rope_t = table(i % 64, i < 64, 64, np.ones(P, f))
    rope_a = table(i % 16, i % 64 < 32, 16, np.where(i % 32 < 16, -1, 1).astype(f))
    xs = np.concatenate([a["x_prompt"][0], a["x_sample"][0]])
    st = np.stack([a["state_ret_fwd"][0, 0], a["state_ret_bwd"][0, 0]])[:, :, dims]
    return {
        "stream": stream, "vec": vec, "cst": cst,
        "x": xs.reshape(T, KT, P).transpose(2, 1, 0),
        "diff": np.broadcast_to(diff[:, :, None], (P, 2, HEADS, P)), "tri": tri, "iota": iota,
        "rope_t": rope_t, "rope_a": rope_a, "mask": mask,
        "state": st.reshape(2, HEADS, 2, P, DV).transpose(1, 3, 0, 2, 4),
        "cache_v": a["cache_attn_v"][0, 0].reshape(NCTX, KVH * HD),
        "cache_k": a["cache_attn_k"][0, 0].transpose(1, 2, 0),
    }, dims


_OUTS = {"y": (KT, P, T), "new_state": (2, HEADS, P, 2, DV), "new_k": (KVH, HD, NCTX), "new_v": (NCTX, KVH * HD)}


def kernel(**inputs):
    import numpy as np
    import concourse.bacc as bacc
    from concourse.bass_utils import run_bass_kernel_spmd as run

    arrays, dims = _layout(inputs)
    arrays = {k: np.ascontiguousarray(x) for k, x in arrays.items()}
    nc = bacc.Bacc("TRN2", target_bir_lowering=False, num_devices=1)
    dr = {k: nc.dram_tensor(k + "_dram", x.shape, F32, kind="ExternalInput").ap() for k, x in arrays.items()}
    for k, shape in _OUTS.items():
        dr[k] = nc.dram_tensor(k + "_dram", shape, F32, kind="ExternalOutput").ap()
    build(nc, dr)
    got = run(nc, [{k + "_dram": x for k, x in arrays.items()}], core_ids=[0]).results[0]
    y = got["y_dram"].reshape(D, T).T
    state = np.empty((2, HEADS, DK, DV), np.float32)
    state[:, :, dims] = got["new_state_dram"].transpose(0, 1, 3, 2, 4).reshape(2, HEADS, DK, DV)
    k = got["new_k_dram"].transpose(2, 0, 1)
    return (np.ascontiguousarray(y[:NCTX])[None], np.ascontiguousarray(y[NCTX:])[None],
            state[0][None, None], state[1][None, None],
            np.ascontiguousarray(k)[None, None], got["new_v_dram"].reshape(1, 1, NCTX, KVH, HD))
```
